# Optimizing a Trainium2 kernel written in Bass

```python
import math
import jax, jax.numpy as jnp
from jax import lax
import numpy as np

D_MODEL = 1024
BATCH = 1
SEQ = 512
DEPTH = 4

N_MIXERS = 3
N_A_LAYERS = (DEPTH + 2) // 3
N_B_LAYERS = (DEPTH + 1) // 3
N_C_LAYERS = DEPTH // 3
HEAD_DIM = 64
EPS = 1e-6

A_GROUPS = ((128, 1), (512, 4), (2048, 16))
A_N_GROUPS = len(A_GROUPS)
A_HEADS = 8
A_BLOCK = 128
A_IN = 3 * A_N_GROUPS * A_HEADS * HEAD_DIM
A_OUT = A_HEADS * HEAD_DIM

B_HEADS = 16
B_KV_HEADS = 4
B_IDX_HEADS = 8
B_IDX_DIM = 64
B_TOPK_MAX = 256
B_BLOCK = 128
B_SPLITS = (B_HEADS * HEAD_DIM, B_KV_HEADS * HEAD_DIM, B_KV_HEADS * HEAD_DIM,
            B_IDX_HEADS * B_IDX_DIM, B_IDX_DIM, B_IDX_HEADS)
B_IN = sum(B_SPLITS)
B_OUT = B_HEADS * HEAD_DIM

C_HEADS = 8
C_KDIM = 128
C_VDIM = 128
C_CONV = 4
C_CHUNK = 64
C_CONV_CH = 2 * C_HEADS * C_KDIM + C_HEADS * C_VDIM
C_SPLITS = (C_CONV_CH, C_HEADS * C_VDIM, C_HEADS, C_HEADS)
C_IN = sum(C_SPLITS)
C_OUT = C_HEADS * C_VDIM

D_FF = 4 * D_MODEL

NUM_BUCKETS = 32
MAX_DISTANCE = 2048
A_BIAS_COLS = A_N_GROUPS * A_HEADS
N_BIAS_COLS = A_BIAS_COLS + B_HEADS

kernel_name = 'hybrid_dilated_dsa_gdn_block'

def rms_norm(x, gain):
    xf = x.astype(jnp.float32)
    y = xf * lax.rsqrt(jnp.mean(xf * xf, axis=-1, keepdims=True) + EPS)
    return (y * gain.astype(jnp.float32)).astype(x.dtype)

def l2_norm(x):
    xf = x.astype(jnp.float32)
    return xf * lax.rsqrt(jnp.sum(xf * xf, axis=-1, keepdims=True) + EPS)

def split_last(t, sizes):
    return jnp.split(t, np.cumsum(sizes)[:-1].tolist(), axis=-1)

def t5_bucket(dist):
    max_exact = NUM_BUCKETS // 2
    d = jnp.maximum(dist, 1).astype(jnp.float32)
    log_part = jnp.log(d / max_exact) / math.log(MAX_DISTANCE / max_exact) * (NUM_BUCKETS - max_exact)
    large = jnp.minimum(max_exact + log_part.astype(jnp.int32), NUM_BUCKETS - 1)
    return jnp.where(dist < max_exact, dist, large)

def squared_relu_mlp(h, w1, w2):
    return jnp.square(jax.nn.relu(h @ w1)) @ w2

def dilated_window_attention(q, k, v, bias_tab, window, dilation):
    B, S, H, Dh = q.shape
    n_back = window // dilation
    sub = S // dilation
    blk = math.gcd(A_BLOCK, sub)
    nb = sub // blk
    width = blk + n_back

    def to_sub(t):
        return t.reshape(B, sub, dilation, H, Dh).transpose(0, 2, 1, 3, 4)

    qs = to_sub(q).reshape(B, dilation, nb, blk, H, Dh)
    pad = ((0, 0), (0, 0), (n_back, 0), (0, 0), (0, 0))
    ks = jnp.pad(to_sub(k), pad)
    vs = jnp.pad(to_sub(v), pad)
    win = jnp.arange(nb)[:, None] * blk + jnp.arange(width)[None, :]
    kb = ks[:, :, win]
    vb = vs[:, :, win]
    logits = jnp.einsum('brnqhd,brnkhd->brnhqk', qs, kb).astype(jnp.float32) * (Dh ** -0.5)
    step = jnp.arange(blk)[:, None] - jnp.arange(width)[None, :] + n_back
    key_sub = win[:, None, :] - n_back
    valid = (step >= 0) & (step <= n_back) & (key_sub >= 0)
    bias = bias_tab[t5_bucket(jnp.maximum(step, 0) * dilation)]
    logits = logits + bias.transpose(2, 0, 1).astype(jnp.float32)
    logits = jnp.where(valid[:, None], logits, -jnp.inf)
    m = jnp.max(logits, axis=-1, keepdims=True)
    p = jnp.exp(logits - m)
    s = jnp.sum(p, axis=-1, keepdims=True)
    o = jnp.einsum('brnhqk,brnkhd->brnqhd', (p / s).astype(v.dtype), vb)
    lse = (m + jnp.log(s))[..., 0]
    o = o.reshape(B, dilation, sub, H, Dh).transpose(0, 2, 1, 3, 4).reshape(B, S, H, Dh)
    lse = lse.transpose(0, 1, 2, 4, 3).reshape(B, dilation, sub, H).transpose(0, 2, 1, 3).reshape(B, S, H)
    return o.astype(jnp.float32), lse

def mixer_a(h, w_in, q_gain, k_gain, w_out, bias_tab):
    B, S, _ = h.shape
    qkv = (h @ w_in).reshape(B, S, 3, A_N_GROUPS, A_HEADS, HEAD_DIM)
    q = rms_norm(qkv[:, :, 0], q_gain)
    k = rms_norm(qkv[:, :, 1], k_gain)
    v = qkv[:, :, 2]
    outs, lses = [], []
    for g, (window, dilation) in enumerate(A_GROUPS):
        o, lse = dilated_window_attention(q[:, :, g], k[:, :, g], v[:, :, g],
                                          bias_tab[:, g * A_HEADS:(g + 1) * A_HEADS], window, dilation)
        outs.append(o)
        lses.append(lse)
    wts = jax.nn.softmax(jnp.stack(lses), axis=0)
    y = jnp.sum(wts[..., None] * jnp.stack(outs), axis=0)
    return y.reshape(B, S, A_OUT).astype(h.dtype) @ w_out

def mixer_b(h, w_in, q_gain, k_gain, w_out, bias_tab):
    B, S, _ = h.shape
    q, k, v, q_idx, k_idx, w_idx = split_last(h @ w_in, B_SPLITS)
    q = rms_norm(q.reshape(B, S, B_HEADS, HEAD_DIM), q_gain)
    k = rms_norm(k.reshape(B, S, B_KV_HEADS, HEAD_DIM), k_gain)
    v = v.reshape(B, S, B_KV_HEADS, HEAD_DIM)
    q_idx = q_idx.reshape(B, S, B_IDX_HEADS, B_IDX_DIM)
    w_idx = w_idx * (B_IDX_HEADS ** -0.5)
    topk = min(B_TOPK_MAX, S // 4)
    nb = S // B_BLOCK
    grp = B_HEADS // B_KV_HEADS
    bidx = jnp.arange(B)[:, None, None]

    def blocks(t):
        return t.reshape(B, nb, B_BLOCK, *t.shape[2:]).swapaxes(0, 1)

    def one_block(args):
        blk_id, qb, qib, wb = args
        t = blk_id * B_BLOCK + jnp.arange(B_BLOCK)
        sc = jnp.einsum('bqhd,bsd->bqhs', qib, k_idx).astype(jnp.float32) * (B_IDX_DIM ** -0.5)
        score = jnp.einsum('bqh,bqhs->bqs', wb.astype(jnp.float32), jax.nn.relu(sc))
        causal = jnp.arange(S)[None, :] <= t[:, None]
        score = jnp.where(causal[None], score, -jnp.inf)
        _, sel = lax.top_k(score, topk)
        valid = sel <= t[None, :, None]
        ks = k[bidx, sel]
        vs = v[bidx, sel]
        qg = qb.reshape(B, B_BLOCK, B_KV_HEADS, grp, HEAD_DIM)
        logits = jnp.einsum('bqhgd,bqkhd->bqhgk', qg, ks).astype(jnp.float32) * (HEAD_DIM ** -0.5)
        dist = jnp.maximum(t[None, :, None] - sel, 0)
        bias = bias_tab[t5_bucket(dist)].astype(jnp.float32)
        bias = bias.reshape(B, B_BLOCK, topk, B_KV_HEADS, grp).transpose(0, 1, 3, 4, 2)
        logits = jnp.where(valid[:, :, None, None, :], logits + bias, -jnp.inf)
        p = jax.nn.softmax(logits, axis=-1)
        o = jnp.einsum('bqhgk,bqkhd->bqhgd', p.astype(vs.dtype), vs)
        return o.reshape(B, B_BLOCK, B_OUT)

    out = lax.map(one_block, (jnp.arange(nb), blocks(q), blocks(q_idx), blocks(w_idx)))
    out = out.swapaxes(0, 1).reshape(B, S, B_OUT)
    return out @ w_out

def chunk_gated_delta_rule(q, k, v, g, beta):
    B, S, H, Dk = q.shape
    Dv = v.shape[-1]
    C = math.gcd(C_CHUNK, S)
    n = S // C

    def chunks(t):
        return t.astype(jnp.float32).reshape(B, n, C, H, -1).transpose(1, 0, 3, 2, 4)

    q, k, v = chunks(q), chunks(k), chunks(v)
    g = g.astype(jnp.float32).reshape(B, n, C, H).transpose(1, 0, 3, 2)
    beta = beta.astype(jnp.float32).reshape(B, n, C, H).transpose(1, 0, 3, 2)
    gc = jnp.cumsum(g, axis=-1)
    diff = gc[..., :, None] - gc[..., None, :]
    lower = jnp.tril(jnp.ones((C, C), dtype=bool))
    strict = jnp.tril(jnp.ones((C, C), dtype=bool), -1)
    decay = jnp.where(lower, jnp.exp(jnp.where(lower, diff, 0.0)), 0.0)
    kb = k * beta[..., None]
    a_mat = jnp.where(strict, jnp.einsum('nbhid,nbhjd->nbhij', kb, k) * decay, 0.0)
    eye = jnp.broadcast_to(jnp.eye(C, dtype=jnp.float32), a_mat.shape)
    t_mat = lax.linalg.triangular_solve(a_mat, eye, left_side=True, lower=True, unit_diagonal=True)
    u = t_mat @ (v * beta[..., None])
    w = t_mat @ (kb * jnp.exp(gc)[..., None])
    qk = jnp.where(lower, jnp.einsum('nbhid,nbhjd->nbhij', q, k) * decay, 0.0)

    def step(state, xs):
        qi, ki, ui, wi, gci, qki = xs
        v_new = ui - wi @ state
        o = (qi * jnp.exp(gci)[..., None]) @ state + qki @ v_new
        g_last = gci[..., -1:]
        state = state * jnp.exp(g_last)[..., None] + jnp.einsum(
            'bhcd,bhce->bhde', ki * jnp.exp(g_last - gci)[..., None], v_new)
        return state, o

    state0 = jnp.zeros((B, H, Dk, Dv), jnp.float32)
    _, o = lax.scan(step, state0, (q, k, u, w, gc, qk))
    return o.transpose(1, 0, 3, 2, 4).reshape(B, S, H, Dv)

def mixer_c(h, w_in, conv_w, a_log, dt_bias, o_gain, w_out):
    B, S, _ = h.shape
    qkv, gate, b, a = split_last(h @ w_in, C_SPLITS)
    xpad = jnp.pad(qkv, ((0, 0), (C_CONV - 1, 0), (0, 0)))
    conv = sum(conv_w[j] * xpad[:, j:j + S] for j in range(C_CONV))
    conv = jax.nn.silu(conv)
    q, k, v = split_last(conv, (C_HEADS * C_KDIM, C_HEADS * C_KDIM, C_HEADS * C_VDIM))
    q = l2_norm(q.reshape(B, S, C_HEADS, C_KDIM)) * (C_KDIM ** -0.5)
    k = l2_norm(k.reshape(B, S, C_HEADS, C_KDIM))
    v = v.reshape(B, S, C_HEADS, C_VDIM)
    beta = jax.nn.sigmoid(b.astype(jnp.float32))
    g = -jnp.exp(a_log.astype(jnp.float32)) * jax.nn.softplus(a.astype(jnp.float32) + dt_bias.astype(jnp.float32))
    o = chunk_gated_delta_rule(q, k, v, g, beta)
    o = rms_norm(o, o_gain) * jax.nn.silu(gate.reshape(B, S, C_HEADS, C_VDIM).astype(jnp.float32))
    return o.reshape(B, S, C_OUT).astype(h.dtype) @ w_out

def setup_inputs(seed: int = 0) -> dict:
    key = jax.random.key(seed)
    ks = jax.random.split(key, 21)

    def nrm(k, shape, scale):
        return jax.random.normal(k, shape, jnp.float32) * scale

    def gain(k, shape):
        return 1.0 + 0.05 * jax.random.normal(k, shape, jnp.float32)

    dt = jnp.exp(jax.random.uniform(ks[20], (N_C_LAYERS, C_HEADS), jnp.float32, math.log(1e-3), math.log(1e-1)))
    return {
        'x': nrm(ks[0], (BATCH, SEQ, D_MODEL), 1.0),
        'rel_bias': nrm(ks[1], (NUM_BUCKETS, N_BIAS_COLS), 0.5),
        'norm_mix': gain(ks[2], (DEPTH, D_MODEL)),
        'norm_mlp': gain(ks[3], (DEPTH, D_MODEL)),
        'mlp_w1': nrm(ks[4], (DEPTH, D_MODEL, D_FF), D_MODEL ** -0.5),
        'mlp_w2': nrm(ks[5], (DEPTH, D_FF, D_MODEL), D_FF ** -0.5),
        'a_w_in': nrm(ks[6], (N_A_LAYERS, D_MODEL, A_IN), D_MODEL ** -0.5),
        'a_q_gain': gain(ks[7], (N_A_LAYERS, HEAD_DIM)),
        'a_k_gain': gain(ks[8], (N_A_LAYERS, HEAD_DIM)),
        'a_w_out': nrm(ks[9], (N_A_LAYERS, A_OUT, D_MODEL), A_OUT ** -0.5),
        'b_w_in': nrm(ks[10], (N_B_LAYERS, D_MODEL, B_IN), D_MODEL ** -0.5),
        'b_q_gain': gain(ks[11], (N_B_LAYERS, HEAD_DIM)),
        'b_k_gain': gain(ks[12], (N_B_LAYERS, HEAD_DIM)),
        'b_w_out': nrm(ks[13], (N_B_LAYERS, B_OUT, D_MODEL), B_OUT ** -0.5),
        'c_w_in': nrm(ks[14], (N_C_LAYERS, D_MODEL, C_IN), D_MODEL ** -0.5),
        'c_conv_w': nrm(ks[15], (N_C_LAYERS, C_CONV, C_CONV_CH), C_CONV ** -0.5),
        'c_a_log': jnp.log(jax.random.uniform(ks[16], (N_C_LAYERS, C_HEADS), jnp.float32, 1.0, 16.0)),
        'c_dt_bias': jnp.log(jnp.expm1(dt)),
        'c_o_gain': gain(ks[17], (N_C_LAYERS, C_VDIM)),
        'c_w_out': nrm(ks[18], (N_C_LAYERS, C_OUT, D_MODEL), C_OUT ** -0.5),
    }

def reference(x, rel_bias, norm_mix, norm_mlp, mlp_w1, mlp_w2,
              a_w_in, a_q_gain, a_k_gain, a_w_out,
              b_w_in, b_q_gain, b_k_gain, b_w_out,
              c_w_in, c_conv_w, c_a_log, c_dt_bias, c_o_gain, c_w_out):
    bias_a = rel_bias[:, :A_BIAS_COLS]
    bias_b = rel_bias[:, A_BIAS_COLS:]
    for i in range(DEPTH):
        kind = i % N_MIXERS
        j = i // N_MIXERS
        h = rms_norm(x, norm_mix[i])
        if kind == 0:
            y = mixer_a(h, a_w_in[j], a_q_gain[j], a_k_gain[j], a_w_out[j], bias_a)
        elif kind == 1:
            y = mixer_b(h, b_w_in[j], b_q_gain[j], b_k_gain[j], b_w_out[j], bias_b)
        else:
            y = mixer_c(h, c_w_in[j], c_conv_w[j], c_a_log[j], c_dt_bias[j], c_o_gain[j], c_w_out[j])
        x = x + y
        x = x + squared_relu_mlp(rms_norm(x, norm_mlp[i]), mlp_w1[i], mlp_w2[i])
    return x


_drawn_inputs = setup_inputs


def setup_inputs(seed=0):
    import zlib

    import numpy as np

    out = dict(_drawn_inputs(seed))
    spreads = {}
    factors = {'a_q_gain': 4.203, 'a_k_gain': 4.045, 'b_q_gain': 8.0, 'b_k_gain': 8.0, 'c_o_gain': 3.905}
    for name, (base, spread) in spreads.items():
        noise = np.random.default_rng([zlib.crc32(name.encode()), seed]).standard_normal(out[name].shape)
        drawn = base * np.exp(spread * noise) if base else spread * noise
        out[name] = __import__('jax').numpy.asarray(drawn.astype(out[name].dtype))
    for name, factor in factors.items():
        out[name] = (out[name] * factor).astype(out[name].dtype)
    return out
```

```python
import math
from contextlib import ExitStack

import concourse.bass as bass
import numpy as np
from concourse import mybir

F32 = mybir.dt.float32
F32R = mybir.dt.float32r
ALU = mybir.AluOpType
ACT = mybir.ActivationFunctionType
AX = mybir.AxisListType

P = 128
TOK = 512
NB = TOK // P
DM = 1024
CT = DM // P
DEPTH = 4
FF = 4 * DM
QUARTERS = FF // DM
CW = 256
EPS = 1e-6
HD = 64
A_HEADS, A_GROUPS = 8, ((128, 1), (512, 4), (2048, 16))
A_PAIRS = A_HEADS // 2
B_HEADS, B_KV, B_IDX = 16, 4, 8
TOPK = 128
C_HEADS = 8
BUCKETS = 32
BIAS_COLS = len(A_GROUPS) * A_HEADS + B_HEADS
MASKED = -1.0e30
TAKEN = -3.0e38
RW = TOK + P
A_BIAS = (256, 512, 512)

G_MIX, G_MLP = 0, DEPTH * CT
G_AQ = 2 * DEPTH * CT
G_AK = G_AQ + 2
G_BQ = G_AK + 2
G_BK = G_BQ + 1
G_CO = G_BK + 1
G_CONV = G_CO + 1
NPARAM = G_CONV + 4 * 3 * C_HEADS
M_ID, M_ONES, M_HALVES = 0, 1, 2
M_CAUSAL, M_DECAY, M_LAST, M_LEVEL = 3, 4, 5, 6
LEVELS = 7
NMASK = M_LEVEL + LEVELS
COMMON_MASKS = 4

KINDS = (0, 1, 2, 0)


def plan():
    chunks = []
    for i in range(DEPTH):
        kind = KINDS[i]
        if kind == 0:
            chunks += [("av", i, v, CT, 1) for v in range(6)]
            chunks += [("aqk", i, c, CT, 2) for c in range(3 * A_PAIRS)]
            chunks += [("out", i, k, 4, 1) for k in range(4)]
        elif kind == 1:
            chunks += [("bkw", i, 0, CT, 4), ("bqi", i, 0, CT, 1), ("bqi", i, 1, CT, 1), ("bv", i, 0, CT, 1)]
            chunks += [("bq", i, c, CT, 4) for c in range(4)] + [("bk", i, 0, CT, 1)]
            chunks += [("out", i, k, CT, 4) for k in range(4)]
        else:
            chunks += [("cab", i, 0, CT, 4)]
            chunks += [("chd", i, c, CT, 2) for c in range(2 * C_HEADS)]
            chunks += [("out", i, k, CT, 1) for k in range(4)]
        chunks += [("mlp", i, c, CT, 1) for c in range(8 * QUARTERS)]
    return chunks


def trunk(nc, x_in, rel_bias, params, c_gates, masks, bucket_rows, bias_mask, mlp_w1, mlp_w2,
          a_w_in, a_w_out, b_w_in, b_w_out, c_w_in, c_w_out, out, layers=range(DEPTH)):
    CHUNKS = [c for c in plan() if c[1] in layers]
    N = len(CHUNKS)
    first_chunk = {}
    for n, c in enumerate(CHUNKS):
        first_chunk.setdefault(c[:2], n)

    raw_value, at = [], [0, 0]
    for n, c in enumerate(CHUNKS):
        at[n % 2] += 16 * c[4]
        raw_value.append(at[n % 2])

    def added(li, mlp):
        return CT * (1 + li * (1 + QUARTERS) + (1 if mlp else 0))

    with ExitStack() as ctx:
        def sb(name, shape, dt=F32):
            return ctx.enter_context(nc.sbuf_tensor(name, shape, dt))

        def sem(name):
            return ctx.enter_context(nc.semaphore(name))

        x = sb("x", [P, CT, TOK])
        h_hi, h_lo = sb("h_hi", [P, CT, TOK], F32R), sb("h_lo", [P, CT, TOK], F32R)
        g_hi, g_lo = sb("g_hi", [P, CT, TOK], F32R), sb("g_lo", [P, CT, TOK], F32R)
        raw = [sb(f"raw{s}", [P, CT, CW]) for s in range(2)]
        w_hi = [sb(f"w_hi{s}", [P, CT, CW], F32R) for s in range(2)]
        w_lo = [sb(f"w_lo{s}", [P, CT, CW], F32R) for s in range(2)]
        par = sb("par", [P, NPARAM])
        com = sb("com", [P, COMMON_MASKS, P])
        eps_col = sb("eps_col", [P, 1])
        ident, ones, halves, causal = (com[:, k, :] for k in range(COMMON_MASKS))
        ARENA = 23400
        arena = sb("arena", [P, ARENA])
        taken = [0]

        def part(n):
            a = arena[:, taken[0]:taken[0] + n]
            taken[0] += n
            assert taken[0] <= ARENA, taken[0]
            return a

        def fresh():
            taken[0] = 0

        fresh()
        sq = [part(TOK) for _ in range(2)]
        ss, rs = part(TOK), part(TOK)
        h32 = [part(TOK) for _ in range(2)]
        relu_t = [part(TOK) for _ in range(2)]
        gsq = [part(TOK) for _ in range(2)]
        x_tok = part(NB * DM).rearrange("p (b n) -> p b n", b=NB)
        bias_rows = part(RW)
        rb_in = part(BIAS_COLS)
        bucket_sb = part(RW)
        bmask_sb = part(RW)

        bank = [ctx.enter_context(nc.psum_tensor(f"bank{k}", [P, TOK], F32)) for k in range(8)]
        lin_bank = bank[0:2]
        stat_bank = bank[7]

        bias_dram = nc.dram_tensor("bias_scratch", [BIAS_COLS, RW], F32, kind="Internal").ap()

        raw_loaded = [sem(f"raw_loaded{s}") for s in range(2)]
        w_hi_done, w_lo_done, lin_done = sem("w_hi_done"), sem("w_lo_done"), sem("lin_done")
        const_loaded, x_loaded = sem("const_loaded"), sem("x_loaded")
        x_turned, x_added = sem("x_turned"), sem("x_added")
        sq_done, ss_added, norm_sum = sem("sq_done"), sem("ss_added"), sem("norm_sum")
        ln_done, rs_done = sem("ln_done"), sem("rs_done")
        h32_done, hh_done, hl_done = sem("h32_done"), sem("hh_done"), sem("hl_done")
        relu_done, gsq_done = sem("relu_done"), sem("gsq_done")
        gh_done, gl_done = sem("gh_done"), sem("gl_done")
        copied = sem("copied")
        qsq_done, q_evac, ssq_done = sem("qsq_done"), sem("q_evac"), sem("ssq_done")
        qln_done, qrs_done, qk_ready = sem("qln_done"), sem("qrs_done"), sem("qk_ready")
        bias_mm, bias_added, bias_saved = sem("bias_mm"), sem("bias_added"), sem("bias_saved")
        bias_loaded = [sem(f"bias_loaded{s}") for s in range(2)]
        s_done, l_done, negmax_done, p_done = sem("s_done"), sem("l_done"), sem("negmax_done"), sem("p_done")
        pt_done, pt_copied, pv_done = sem("pt_done"), sem("pt_copied"), sem("pv_done")
        rinv_done, y_done = sem("rinv_done"), sem("y_done")
        yh_done, yl_done = sem("yh_done"), sem("yl_done")
        iw_turned, iw_ready = sem("iw_turned"), sem("iw_ready")
        idx_done, idx_relu, idx_acc = sem("idx_done"), sem("idx_relu"), sem("idx_acc")
        topk_step, mask_ready, tm_done = sem("topk_step"), sem("mask_ready"), sem("tm_done")
        scaled = sem("scaled")
        out_turned, out_copied, out_saved = sem("out_turned"), sem("out_copied"), sem("out_saved")

        gate_step, gate_ln, gates_ready = sem("gate_step"), sem("gate_ln"), sem("gates_ready")
        gate_exp, cols_turned, cols_copied = sem("gate_exp"), sem("cols_turned"), sem("cols_copied")
        last_spread, cmask_loaded, col_exp = sem("last_spread"), sem("cmask_loaded"), sem("col_exp")
        conv_step, conv_done, tanh_done, silu_done = sem("conv_step"), sem("conv_done"), sem("tanh_done"), sem("silu_done")
        csq_done, csum_done, cln_done, crs_done = sem("csq_done"), sem("csum_done"), sem("cln_done"), sem("crs_done")
        qkn_done, rows_spread, age_done = sem("qkn_done"), sem("rows_spread"), sem("age_done")
        decay_done, grow_done, qe_done = sem("decay_done"), sem("grow_done"), sem("qe_done")
        kk_done, kv_turned, kv_scaled = sem("kk_done"), sem("kv_turned"), sem("kv_scaled")
        at_raw, at_done, atl_done = sem("at_raw"), sem("at_done"), sem("atl_done")
        u_done, t_turned, t_init, t_done = sem("u_done"), sem("t_turned"), sem("t_init"), sem("t_done")
        w_done, w_copied, tw_done = sem("w_done"), sem("w_copied"), sem("tw_done")
        wt_done, wt_copied = sem("wt_done"), sem("wt_copied")
        vn_done, vn_copied, ds_done, state_done = sem("vn_done"), sem("vn_copied"), sem("ds_done"), sem("state_done")
        o_done, osq_done, osum_done, oln_done, ors_done = (sem("o_done"), sem("osq_done"), sem("osum_done"),
                                                           sem("oln_done"), sem("ors_done"))
        on_done, y32_done = sem("on_done"), sem("y32_done")

        units, heads, y_first = [], [], {}
        counts = dict(s=0, t=0, v=0, y=0, tm=0)
        value = [0, 0]
        for li, i in enumerate(layers):
            y_first[i] = counts["y"]
            if KINDS[i] == 2:
                counts["y"] += C_HEADS
                continue
            kind = KINDS[i]
            for f in range(A_PAIRS if kind == 0 else B_HEADS // 2):
                for half in range(2):
                    head = 2 * f + half if kind == 0 else 8 * (f // 4) + f % 4 + 4 * half
                    H = len(heads)
                    value[H % 2] += 16 * (3 if kind == 0 else 1)
                    heads.append(dict(i=i, kind=kind, head=head, loaded=value[H % 2], f=f))
                    for b in (3, 0, 2, 1):
                        u = dict(i=i, kind=kind, f=f, half=half, head=head, b=b, H=H, u=len(units), s0=counts["s"],
                                 t0=counts["t"], v0=counts["v"])
                        if kind == 0:
                            k0 = max(0, b - 1)
                            u["pieces"] = [(0, k0, b + 1)] + [(g, 0, b + 1) for g in (1, 2)]
                        else:
                            u["pieces"] = [(0, 0, b + 1)]
                            u["tm"] = counts["tm"] if b else None
                            counts["tm"] += b > 0
                        u["blocks"] = [(g, kb) for g, ka, kz in u["pieces"] for kb in range(ka, kz)]
                        u["tp"] = -(-len(u["blocks"]) // 4)
                        counts["s"] += len(u["pieces"])
                        counts["t"] += u["tp"]
                        counts["v"] += u["tp"]
                        units.append(u)
                    heads[H]["s_end"] = counts["s"]
                heads[-1]["yt"] = counts["t"]
                heads[-1]["ylast"] = len(units)
                heads[-1]["y"] = counts["y"]
                counts["t"] += 1
                counts["y"] += 1
        last_piece_user = {u["tm"]: u["s0"] + 1 for u in units if u.get("tm") is not None}
        SKEW = {0: 1, 1: 2}

        def units_of(i):
            return [u for u in units if u["i"] == i]

        def pair_of(i, f):
            return next(h for h in heads if h["i"] == i and h["f"] == f and "yt" in h)

        q_first, copy_first, at_q, at_c = {}, {}, 0, 0
        for i in layers:
            q_first[i], copy_first[i] = at_q, at_c
            at_q += {0: 6 * A_PAIRS, 1: 10, 2: 0}[KINDS[i]]
            at_c += {0: 12, 1: 8, 2: 2 + 4 * C_HEADS}[KINDS[i]]

        evac = []
        for n, c in enumerate(CHUNKS):
            stage, i = c[:2]
            li = list(layers).index(i)
            for j in range(2):
                k = 2 * (n - first_chunk[stage, i]) + j
                if stage == "out":
                    evac.append((x_added, added(li, False) + k + 1))
                elif stage == "mlp":
                    q, k = divmod(k, 16)
                    evac.append((None, None) if k < 8 else (x_added, added(li, True) + 8 * q + k - 8 + 1))
                elif stage == "av":
                    evac.append((copied, copy_first[i] + k + 1))
                elif stage in ("aqk", "bq"):
                    evac.append((q_evac, q_first[i] + k + 1))
                elif stage == "bk":
                    evac.append((q_evac, q_first[i] + 8 + k + 1))
                elif stage in ("bkw", "bqi", "bv"):
                    evac.append((copied, copy_first[i] + k + {"bkw": 0, "bqi": 2, "bv": 6}[stage] + 1))
                elif stage == "cab":
                    evac.append((copied, copy_first[i] + k + 1))
                else:
                    evac.append((copied, copy_first[i] + 2 + k + 1))

        fresh()
        aq = [[part(TOK) for _ in range(6)] for _ in range(2)]
        av = part(NB * 3 * 512).rearrange("p (b n) -> p b n", b=NB)
        ay = part(NB * P).rearrange("p (b n) -> p b n", b=NB)
        abias = [part(sum(A_BIAS)) for _ in range(2)]
        al = [part(1280), part(768)]
        apt = [part(512) for _ in range(2)]
        asq, ars = part(TOK), part(TOK)
        ayf = part(TOK)
        small = sb("small", [P, 40])
        fresh()
        bq = [part(TOK) for _ in range(8)]
        bk = [part(TOK) for _ in range(2)]
        bv = part(NB * CW).rearrange("p (b n) -> p b n", b=NB)
        by = part(NB * P).rearrange("p (b n) -> p b n", b=NB)
        bbias = [part(TOK) for _ in range(2)]
        bl = [part(TOK) for _ in range(3)]
        bpt = [part(512) for _ in range(2)]
        bsq, brs = part(TOK), part(TOK)
        byf = part(TOK)
        bqi = [part(TOK) for _ in range(4)]
        bki = part(TOK)
        bw_row = part(TOK)
        bw = part(NB * B_IDX).rearrange("p (b n) -> p b n", b=NB)
        score = {b: part(P * (b + 1)) for b in (1, 2, 3)}
        brelu = [part(TOK) for _ in range(2)]
        btm = [part(TOK) for _ in range(2)]
        best = part(8)

        fresh()
        gc_row, beta_row = part(TOK), part(TOK)
        head_sel = part(C_HEADS * P).rearrange("p (h n) -> p h n", h=C_HEADS)
        cmask = part((NMASK - M_DECAY) * P).rearrange("p (k n) -> p k n", n=P)
        gate_in = part(2)
        neg_a = part(1)

        def cols():
            return part(NB * C_HEADS).rearrange("p (c h) -> p c h", c=NB)

        gc_col, beta_col, g_last, e_last, k_decay, beta_g = (cols() for _ in range(6))
        cx = [part(TOK) for _ in range(2)]
        cy = [[part(TOK) for _ in range(3)] for _ in range(2)]
        cg = [part(TOK) for _ in range(2)]
        cth = [part(TOK) for _ in range(2)]
        csq = [part(TOK) for _ in range(2)]
        crs = [part(TOK) for _ in range(2)]
        ors = part(TOK)

        def four():
            return part(TOK).rearrange("p (c n) -> p c n", c=NB)

        qn, kn, qe, grow, decay, qkd, at = (four() for _ in range(7))
        atl = [four() for _ in range(3)]
        Tm, Um, Wm = four(), four(), four()
        v_beta, k_beta, k_dec, wt = four(), four(), four(), four()
        on, cyo = part(TOK), part(TOK)
        vn = [part(P) for _ in range(2)]
        state = part(P)
        m_decay, m_last = cmask[:, 0, :], cmask[:, 1, :]
        m_level = [cmask[:, 2 + k, :] for k in range(LEVELS)]
        gz, ge, gu, gl_, gd, gr = (m.rearrange("p c n -> p (c n)")[0:C_HEADS, :] for m in (*atl, Tm, Um, Wm))

        def by_block(m):
            return m.rearrange("p (b n) -> p b n", b=NB)

        def reversed_blocks(m):
            return by_block(m)[:, :, ::-1]

        def bk4(k):
            return bank[k][:].rearrange("p (c n) -> p c n", c=NB)

        def halves_of(m, k, second):
            v = m.rearrange("p c (b z s) -> p c b z s", z=2, s=1 << k)
            return v[:, :, :, 1 if second else 0, :]

        def packed(bank_k, k):
            return bank[bank_k][:, 0:NB * 64].rearrange("p (c b s) -> p c b s", c=NB, s=1 << k)

        FILL = dict(sums=12, products=24, t=28, wt=67, vn=(69, 74, 79, 84), ds=(72, 77, 82, 90), osum=96)
        FILL_W = {k: 28 + 6 * k - 3 for k in range(1, 7)}
        FILL_TW = {k: 28 + 6 * k for k in range(1, 7)}

        mem = {0: dict(y=ay, l=al, pt=apt, sq=asq, rs=ars, yf=ayf, bias=abias),
               1: dict(y=by, l=bl, pt=bpt, sq=bsq, rs=brs, yf=byf, bias=bbias)}
        mx = [small[:, 4 * k:4 * k + 3] for k in range(4)]
        negmax = [small[:, 16 + k:17 + k] for k in range(4)]
        psum_of = [small[:, 20 + k:21 + k] for k in range(4)]
        rinv = [small[:, 24 + k:25 + k] for k in range(4)]

        def l_of(u):
            ring = mem[u["kind"]]["l"]
            return ring[u["u"] % len(ring)]

        def bias_of(u, g, ka, kz):
            if u["kind"] == 1 and u["b"]:
                return btm[u["tm"] % 2][:, 0:P * (kz - ka)]
            t = mem[u["kind"]]["bias"][u["H"] % 2]
            off = (0, 256, 768)[g] if u["kind"] == 0 else 0
            end = off + (A_BIAS[g] if u["kind"] == 0 else TOK)
            return t[:, end - P * (kz - ka):end]

        def qk_of(u, g):
            rows = slice(HD * u["half"], HD * u["half"] + HD)
            if u["kind"] == 0:
                q, k = aq[u["f"] % 2][2 * g], aq[u["f"] % 2][2 * g + 1]
            else:
                q, k = bq[u["f"]], bk[u["f"] // 4]
            return q[rows, :], k[rows, :]

        def v_of(u, g, kb):
            if u["kind"] == 0:
                c = (g * A_HEADS + u["head"]) * HD
                return av[:, kb, c:c + HD]
            c = (u["head"] // (B_HEADS // B_KV)) * HD
            return bv[:, kb, c:c + HD]

        def tanh_index(h, k):
            if k == 3:
                return 4 * h + 3 + (3 if h + 1 < C_HEADS else 0)
            return k if h == 0 else 4 * h - 1 + k

        def rank_in_ring(u):
            n = len(mem[u["kind"]]["l"])
            p = u["u"] - n
            return units[p] if p >= 0 and units[p]["i"] == u["i"] else None

        block = ctx.enter_context(nc.Block())

        @block.sync
        def _(sp):
            def load(n, k, dst, src):
                sp.dma_start(dst, src).then_inc(raw_loaded[n % 2], 16)

            def rows(w, c0, cols, kt=CT, r0=0):
                return w[r0:r0 + kt * P, c0:c0 + cols].rearrange("(k p) n -> p k n", p=P)

            def chunk(n):
                stage, i, k, kt, _ = CHUNKS[n]
                r = raw[n % 2]
                if n >= 2:
                    sp.wait_ge(w_lo_done, n - 1)
                if stage == "av":
                    load(n, 0, r[:], rows(a_w_in[i // 3], 3072 + k * CW, CW))
                elif stage == "aqk":
                    f, g = divmod(k, 3)
                    for s in range(2):
                        load(n, s, r[:, :, P * s:P * s + P], rows(a_w_in[i // 3], 1536 * s + 512 * g + P * f, P))
                elif stage == "out" and KINDS[i] == 1:
                    for z in range(2):
                        for s in range(2):
                            r0 = (8 * z + 4 * s) * HD
                            src = b_w_out[0][r0:r0 + 4 * HD, k * CW:(k + 1) * CW].rearrange("(t p) n -> p t n", p=HD)
                            load(n, 2 * z + s, r[HD * s:HD * s + HD, 4 * z:4 * z + 4, :], src)
                elif stage == "out":
                    w = {0: a_w_out, 1: b_w_out, 2: c_w_out}[KINDS[i]][i // 3]
                    load(n, 0, r[:, 0:kt, :], rows(w, k * CW, CW, kt))
                elif stage == "cab":
                    w = c_w_in[0]
                    for s in range(2):
                        load(n, 0, r[:, :, P * s:P * s + 8], rows(w, 4096 + 8 * s, 8))
                        load(n, 0, r[:, :, P * s + 8:P * s + P], rows(w, 0, P - 8))
                elif stage == "chd":
                    for s in range(2):
                        load(n, s, r[:, :, P * s:P * s + P], rows(c_w_in[0], DM * (2 * (k % 2) + s) + P * (k // 2), P))
                elif stage == "bkw":
                    w = b_w_in[0]
                    for s in range(2):
                        load(n, s, r[:, :, HD * s:HD * s + HD], rows(w, 2048, HD))
                    load(n, 2, r[:, :, P:P + 8], rows(w, 2112, 8))
                    load(n, 3, r[:, :, P + 8:CW], rows(w, 0, P - 8))
                elif stage == "bqi":
                    load(n, 0, r[:], rows(b_w_in[0], 1536 + k * CW, CW))
                elif stage == "bv":
                    load(n, 0, r[:], rows(b_w_in[0], 1280, CW))
                elif stage == "bk":
                    load(n, 0, r[:], rows(b_w_in[0], 1024, CW))
                elif stage == "bq":
                    for t in range(2):
                        a = 8 * (k // 2) + 2 * (k % 2) + t
                        for s in range(2):
                            c = P * t + HD * s
                            load(n, 2 * t + s, r[:, :, c:c + HD], rows(b_w_in[0], (a + 4 * s) * HD, HD))

            def mlp_chunks(i, n0, q):
                c_up = [sp.snap(q * DM + k * CW) if not isinstance(q, int) else q * DM + k * CW for k in range(4)]
                r_down = c_up[0]
                free = [sp.snap(q * 8 + (n0 + k - 1)) if not isinstance(q, int) else q * 8 + n0 + k - 1
                        for k in range(8)]
                for k in range(8):
                    if k < 4:
                        src = mlp_w1[i][:, bass.ds(c_up[k], CW)]
                    else:
                        src = mlp_w2[i][bass.ds(r_down, DM), (k - 4) * CW:(k - 3) * CW]
                    src = src.rearrange("(k p) n -> p k n", p=P)
                    if isinstance(q, int) and free[k] < 1:
                        pass
                    else:
                        sp.wait_ge(w_lo_done, free[k])
                    load(n0 + k, 0, raw[(n0 + k) % 2][:], src)

            sp.dma_start(com[:], masks[0:COMMON_MASKS * P, :].rearrange("(k p) n -> p k n", p=P)).then_inc(const_loaded, 16)
            for b in range(NB):
                sp.dma_start(x_tok[:, b, :], x_in[b * P:(b + 1) * P, :]).then_inc(x_loaded, 16)
            sp.dma_start(par[:], params).then_inc(const_loaded, 16)
            sp.dma_start(bucket_sb[0:BUCKETS, :], bucket_rows).then_inc(const_loaded, 16)
            sp.dma_start(rb_in[0:BUCKETS, :], rel_bias).then_inc(const_loaded, 16)
            sp.dma_start(bmask_sb[0:BIAS_COLS, :], bias_mask).then_inc(const_loaded, 16)
            for i in layers:
                n = min(first_chunk[s, j] for s, j in first_chunk if j == i)
                n_mlp = first_chunk["mlp", i]
                for k in range(n, n_mlp):
                    chunk(k)
                with sp.Fori(0, QUARTERS) as q:
                    mlp_chunks(i, n_mlp, q)
            for b in range(NB):
                sp.wait_ge(out_copied, 2 * b + 2)
                sp.dma_start(out[b * P:(b + 1) * P, :], x_tok[:, b, :]).then_inc(out_saved, 16)
            sp.wait_ge(out_saved, 16 * NB)

        @block.gpsimd
        def _(pool):
            def split(n, kt, value=None):
                value = n + 1 if value is None else value
                pool.wait_ge(w_hi_done, value)
                s = n % 2
                nc.gpsimd.tensor_tensor(w_lo[s][:, 0:kt, :], raw[s][:, 0:kt, :], w_hi[s][:, 0:kt, :].bitcast(F32),
                                        ALU.subtract).then_inc(w_lo_done, 1)

            def split_ahead(m):
                if m + 2 < N:
                    split(m + 2, CHUNKS[m + 2][3])

            def qk_scale(kind, Q, dst):
                pool.wait_ge(qrs_done, Q + 1)
                nc.gpsimd.tensor_tensor(dst, dst, mem[kind]["rs"], ALU.mult).then_inc(qk_ready, 1)

            def mixer_a(i):
                n0, n1, Q = first_chunk["av", i], first_chunk["aqk", i], q_first[i]
                for v in range(6):
                    split_ahead(n0 + v)
                for k in range(6):
                    if k:
                        qk_scale(0, Q + k - 1, aq[0][k - 1])
                    if k % 2:
                        split_ahead(n1 + k // 2)
                qk_scale(0, Q + 5, aq[0][5])
                for f in range(A_PAIRS - 1):
                    Q1, n2 = Q + 6 * (f + 1), n1 + 3 * (f + 1)
                    for k in range(7):
                        if k:
                            qk_scale(0, Q1 + k - 1, aq[(f + 1) % 2][k - 1])
                        if k % 2 and k < 6:
                            split_ahead(n2 + k // 2)

            def mixer_b(i):
                n0, Q = first_chunk["bkw", i], q_first[i]
                for k in range(4):
                    split_ahead(n0 + k)
                dst = bq + bk
                for k in range(10):
                    if k:
                        qk_scale(1, Q + k - 1, dst[k - 1])
                    if k % 2:
                        split_ahead(n0 + 4 + k // 2)
                qk_scale(1, Q + 9, dst[9])
                for u in units_of(i):
                    if u["b"] == 0:
                        continue
                    t = u["tm"]
                    h = heads[u["H"]]
                    pool.wait_ge(bias_loaded[u["H"] % 2], h["loaded"])
                    pool.wait_ge(mask_ready, 4 - u["b"])
                    if t >= 2:
                        pool.wait_ge(l_done, last_piece_user[t - 2])
                    n = P * (u["b"] + 1)
                    nc.gpsimd.tensor_tensor(btm[t % 2][:, 0:n], bbias[u["H"] % 2][:, TOK - n:TOK],
                                            score[u["b"]], ALU.add).then_inc(tm_done, 1)

            def mixer_c(i):
                n0 = first_chunk["cab", i]
                for k in range(3):
                    split_ahead(n0 + k)
                for h in range(C_HEADS):
                    pool.wait_ge(at_done, h + 1)
                    for k in range(LEVELS):
                        if k >= 3:
                            pool.wait_ge(w_done, 6 * h + k - 3)
                        if k == 3:
                            pool.wait_ge(u_done, 7 * h + 1)
                        nc.gpsimd.tensor_tensor(atl[k % 3], at, m_level[k].unsqueeze(1).to_broadcast([P, NB, P]),
                                                ALU.mult).then_inc(atl_done, 1)
                        if k == 4 and h + 1 < C_HEADS:
                            split_ahead(n0 + 3 + 2 * h)
                    if h + 1 < C_HEADS:
                        split_ahead(n0 + 4 + 2 * h)

            nc.gpsimd.memset(eps_col[:], EPS).then_inc(scaled, 1)
            for n in range(2):
                split(n, CHUNKS[n][3])
            for i in layers:
                (mixer_a, mixer_b, mixer_c)[KINDS[i]](i)
                for k in range(4):
                    split_ahead(first_chunk["out", i] + k)
                n = first_chunk["mlp", i]
                with pool.Fori(0, QUARTERS - 1) as q:
                    for k in range(8):
                        split(n + k, CT, q * 8 + (n + k + 3))
                for k in range(8):
                    split_ahead(n + 8 * (QUARTERS - 1) + k)

        @block.scalar
        def _(act):
            def rounding(n, kt, raw_v=None, lin_v=None):
                s = n % 2
                raw_v = raw_value[n] if raw_v is None else raw_v
                lin_v = 2 * n - 2 if lin_v is None else lin_v
                act.wait_ge(raw_loaded[s], raw_v)
                if not isinstance(lin_v, int) or lin_v > 0:
                    act.wait_ge(lin_done, lin_v)
                nc.scalar.activation(w_hi[s][:, 0:kt, :], raw[s][:, 0:kt, :], ACT.Copy).then_inc(w_hi_done, 1)

            def round_ahead(m):
                if m + 2 < N:
                    rounding(m + 2, CHUNKS[m + 2][3])

            def square_x(m, c, x0):
                act.wait_ge(x_added, x0 + c + 1)
                if c >= 2:
                    act.wait_ge(ss_added, 7 * m + max(1, c - 2))
                nc.scalar.activation(sq[c % 2], x[:, c, :], ACT.Square).then_inc(sq_done, 1)

            def norm(m):
                act.wait_ge(norm_sum, m + 1)
                nc.scalar.activation(rs, stat_bank[:], ACT.Ln, bias=eps_col[:], scale=1.0 / DM).then_inc(ln_done, 1)
                act.wait_ge(ln_done, m + 1)
                nc.scalar.activation(rs, rs, ACT.Exp, scale=-0.5).then_inc(rs_done, 1)
                for c in range(CT):
                    act.wait_ge(h32_done, 8 * m + c + 1)
                    nc.scalar.activation(h_hi[:, c, :], h32[c % 2], ACT.Copy).then_inc(hh_done, 1)

            def residual(n0, x0, m, kt):
                for k in range(4):
                    for c in (2 * k, 2 * k + 1):
                        if m is not None:
                            square_x(m, c, x0)
                    round_ahead(n0 + k)

            def mlp(li, i, m):
                n = first_chunk["mlp", i]
                T, G, X = 2 * n, 8 * QUARTERS * li, added(li, True)
                with act.Fori(0, QUARTERS - 1) as q:
                    t0 = [act.snap(q * 16 + (T + k)) for k in range(0, 17)]
                    g0 = {k: act.snap(q * 8 + (G + k)) for k in range(1, 9)}

                    def ahead(k):
                        v = act.snap(q * 64 + raw_value[n + k + 2])
                        rounding(n + k + 2, CT, v, t0[2 * k + 2])

                    for k in range(4):
                        for j in (2 * k, 2 * k + 1):
                            act.wait_ge(lin_done, t0[j + 1])
                            nc.scalar.activation(relu_t[j % 2], lin_bank[j % 2][:], ACT.Relu).then_inc(relu_done, 1)
                            act.wait_ge(gsq_done, g0[j + 1])
                            nc.scalar.activation(g_hi[:, j, :], gsq[j % 2], ACT.Copy).then_inc(gh_done, 1)
                        ahead(k)
                    for k in range(4, 8):
                        ahead(k)
                q = QUARTERS - 1
                T, G, X, n = T + 16 * q, G + 8 * q, X + 8 * q, n + 8 * q
                for k in range(4):
                    for j in (2 * k, 2 * k + 1):
                        act.wait_ge(lin_done, T + j + 1)
                        nc.scalar.activation(relu_t[j % 2], lin_bank[j % 2][:], ACT.Relu).then_inc(relu_done, 1)
                        act.wait_ge(gsq_done, G + j + 1)
                        nc.scalar.activation(g_hi[:, j, :], gsq[j % 2], ACT.Copy).then_inc(gh_done, 1)
                    round_ahead(n + k)
                residual(n + 4, X, m, CT)

            def copy_tile(t, dst, src, **kw):
                act.wait_ge(lin_done, t + 1)
                nc.scalar.activation(dst, src, ACT.Copy, **kw).then_inc(copied, 1)

            def qk_tile(kind, t, Q, dst, gain, query):
                src, blocks = lin_bank[t % 2][:], lambda m: m
                if query:
                    src, blocks = reversed_blocks(src), by_block
                act.wait_ge(lin_done, t + 1)
                if Q:
                    act.wait_ge(ssq_done, Q)
                nc.scalar.activation(blocks(mem[kind]["sq"]), src, ACT.Square).then_inc(qsq_done, 1)
                nc.scalar.activation(blocks(dst), src, ACT.Copy, scale=par[:, gain:gain + 1]).then_inc(q_evac, 1)

            def qk_rms(kind, Q):
                r = mem[kind]["rs"]
                act.wait_ge(ssq_done, Q + 1)
                if Q:
                    act.wait_ge(qk_ready, Q)
                nc.scalar.activation(r, stat_bank[:], ACT.Ln, bias=eps_col[:], scale=1.0 / HD).then_inc(qln_done, 1)
                act.wait_ge(qln_done, Q + 1)
                nc.scalar.activation(r, r, ACT.Exp, scale=-0.5).then_inc(qrs_done, 1)

            def load_bias(H):
                h = heads[H]
                dst = mem[h["kind"]]["bias"][H % 2]
                if h["kind"] == 0:
                    parts = [(g * A_HEADS + h["head"], (0, 256, 768)[g], A_BIAS[g]) for g in range(3)]
                else:
                    parts = [(3 * A_HEADS + h["head"], 0, TOK)]
                for row, off, n in parts:
                    src = bass.AP(bias_dram.tensor, row * RW + TOK - n, [[1, P], [1, n]])
                    nc.scalar.dma_start(dst[:, off:off + n], src).then_inc(bias_loaded[H % 2], 16)

            def probs(u):
                act.wait_ge(negmax_done, u["u"] + 1)
                n = P * len(u["blocks"])
                L = l_of(u)[:, 0:n]
                k = u["u"] % 4
                nc.scalar.activation(L, L, ACT.Exp, bias=negmax[k], accum_out=psum_of[k]).then_inc(p_done, 1)
                H = u["H"]
                if u["b"] == 1 and H + 2 < len(heads) and heads[H + 2]["i"] == u["i"]:
                    act.wait_ge(l_done, heads[H]["s_end"])
                    load_bias(H + 2)

            def y_round(h):
                act.wait_ge(pt_copied, h["yt"] + 1)
                nc.scalar.activation(g_hi[:, h["f"], :], mem[h["kind"]]["yf"], ACT.Copy).then_inc(yh_done, 1)

            def first_heads(i):
                Hs = [H for H, h in enumerate(heads) if h["i"] == i][:2]
                for H in Hs:
                    load_bias(H)

            def mixer_a(i):
                n0, n1, Q, U = first_chunk["av", i], first_chunk["aqk", i], q_first[i], units_of(i)
                first_heads(i)
                for v in range(6):
                    for j in range(2):
                        t = 2 * (n0 + v) + j
                        copy_tile(t, av[:, 2 * j:2 * j + 2, v * CW:(v + 1) * CW],
                                  lin_bank[t % 2][:].rearrange("p (b n) -> p b n", b=2))
                    round_ahead(n0 + v)
                gains = [(G_AQ, G_AK)[k % 2] + i // 3 for k in range(6)]
                for k in range(6):
                    if k:
                        qk_rms(0, Q + k - 1)
                    qk_tile(0, 2 * n1 + k, Q + k, aq[0][k], gains[k], k % 2 == 0)
                    if k % 2:
                        round_ahead(n1 + k // 2)
                qk_rms(0, Q + 5)
                for f in range(A_PAIRS):
                    Q1, n2 = Q + 6 * (f + 1), n1 + 3 * (f + 1)
                    more = f + 1 < A_PAIRS
                    for k in range(8):
                        probs(U[8 * f + k])
                        if more and 1 <= k <= 6:
                            qk_rms(0, Q1 + k - 1)
                        if more and k < 6:
                            qk_tile(0, 2 * n2 + k, Q1 + k, aq[(f + 1) % 2][k], gains[k], k % 2 == 0)
                            if k % 2:
                                round_ahead(n2 + k // 2)
                        if k == 1 and f:
                            y_round(pair_of(i, f - 1))
                y_round(pair_of(i, A_PAIRS - 1))

            def copy_pieces(u):
                for p in range(u["tp"]):
                    n = P * min(4, len(u["blocks"]) - 4 * p)
                    t = u["t0"] + p
                    act.wait_ge(pt_done, t + 1)
                    v = u["v0"] + p
                    if v >= 2:
                        act.wait_ge(pv_done, v - 1)
                    nc.scalar.activation(mem[u["kind"]]["pt"][v % 2][:, 0:n], bank[4 + t % 2][:, 0:n],
                                         ACT.Copy).then_inc(pt_copied, 1)

            def mixer_b(i):
                n0, Q, U = first_chunk["bkw", i], q_first[i], units_of(i)
                t0 = 2 * n0
                first_heads(i)
                copy_tile(t0, bki, lin_bank[t0 % 2][:])
                copy_tile(t0 + 1, by_block(bw_row[0:B_IDX, :]), reversed_blocks(lin_bank[1][0:B_IDX, :]),
                          scale=float(B_IDX) ** -0.5)
                round_ahead(n0)
                for k in range(4):
                    copy_tile(t0 + 2 + k, by_block(bqi[k]), reversed_blocks(lin_bank[k % 2][:]))
                    if k % 2:
                        round_ahead(n0 + 1 + k // 2)
                    if k == 0:
                        act.wait_ge(iw_turned, 1)
                        nc.scalar.activation(bw.rearrange("p b n -> p (b n)"), bank[4][:, 0:NB * B_IDX],
                                             ACT.Copy).then_inc(iw_ready, 1)
                dst = bq + bk
                for k in range(12):
                    t = t0 + 6 + k
                    if k < 6:
                        for p in range(4 * k, 4 * k + 4):
                            act.wait_ge(idx_done, p + 1)
                            if p >= 2:
                                act.wait_ge(idx_acc, p - 1)
                            n = P * (3 - p // 8 + 1)
                            nc.scalar.activation(brelu[p % 2][:, 0:n], bank[2 + p % 2][:, 0:n], ACT.Relu,
                                                 scale=HD ** -0.5).then_inc(idx_relu, 1)
                            if p % 4 == 1 and k >= 3:
                                qk_rms(1, Q + k - 3)
                    elif k >= 3:
                        qk_rms(1, Q + k - 3)
                    if k < 2:
                        copy_tile(t, bv[:, 2 * k:2 * k + 2, :], lin_bank[t % 2][:].rearrange("p (b n) -> p b n", b=2))
                    else:
                        qk_tile(1, t, Q + k - 2, dst[k - 2], G_BQ if k < 10 else G_BK, k < 10)
                    if k % 2:
                        round_ahead(n0 + 3 + k // 2)
                qk_rms(1, Q + 9)
                for s in range(len(U) + SKEW[1]):
                    if s < len(U):
                        probs(U[s])
                    if s >= SKEW[1]:
                        if (s - SKEW[1]) % 8 == 0 and s > SKEW[1]:
                            y_copy_round(pair_of(i, (s - SKEW[1]) // 8 - 1))
                        copy_pieces(U[s - SKEW[1]])
                y_copy_round(pair_of(i, 7))

            def y_copy_round(h):
                act.wait_ge(pt_done, h["yt"] + 1)
                if h["y"]:
                    act.wait_ge(yl_done, h["y"])
                nc.scalar.activation(by_block(byf), reversed_blocks(bank[4 + h["yt"] % 2][:]), ACT.Copy).then_inc(pt_copied, 1)
                y_round(h)

            def c_copy(i, h, k):
                act.wait_ge(lin_done, 2 * first_chunk["chd", i] + 4 * h + k + 1)
                b = lin_bank[k % 2][:]
                if k < 3:
                    t = 3 * h + k
                    if t >= 2:
                        act.wait_ge(conv_done, t - 1)
                    nc.scalar.activation(cx[t % 2], b, ACT.Copy).then_inc(copied, 1)
                else:
                    nc.scalar.activation(cg[h % 2], b, ACT.Copy, scale=0.5).then_inc(copied, 1)

            def c_tanh(i, items):
                for h, k in items:
                    n = tanh_index(h, k)
                    if n >= 2:
                        act.wait_ge(silu_done, n - 1)
                    if k < 3:
                        act.wait_ge(conv_done, 3 * h + k + 1)
                        src = cy[h % 2][k]
                    else:
                        act.wait_ge(copied, copy_first[i] + 2 + 4 * h + 4)
                        src = cg[h % 2]
                    nc.scalar.activation(cth[n % 2], src, ACT.Tanh).then_inc(tanh_done, 1)

            def mixer_c(i):
                n0, n1 = first_chunk["cab", i], first_chunk["chd", i]
                t0 = 2 * n0
                C8 = slice(0, C_HEADS)
                act.dma_start(cmask, masks[M_DECAY * P:, :].rearrange("(k p) n -> p k n", p=P)).then_inc(cmask_loaded, 16)
                act.dma_start(gate_in[C8, :], c_gates).then_inc(cmask_loaded, 16)
                act.wait_ge(lin_done, t0 + 1)
                nc.scalar.activation(beta_row[C8, :], lin_bank[0][C8, :], ACT.Tanh, scale=0.5).then_inc(copied, 1)
                act.wait_ge(cmask_loaded, 32)
                act.wait_ge(lin_done, t0 + 2)
                nc.scalar.activation(gz, lin_bank[1][C8, :], ACT.Identity, bias=gate_in[C8, 1:2]).then_inc(copied, 1)
                round_ahead(n0)
                act.wait_ge(copied, copy_first[i] + 2)
                nc.scalar.activation(ge, gz, ACT.Abs).then_inc(gate_exp, 1)
                act.wait_ge(gate_exp, 1)
                nc.scalar.activation(ge, ge, ACT.Exp, scale=-1.0).then_inc(gate_exp, 1)
                nc.scalar.activation(neg_a[C8, :], gate_in[C8, 0:1], ACT.Exp).then_inc(gate_exp, 1)
                act.wait_ge(gate_ln, 1)
                nc.scalar.activation(gl_, gu, ACT.Ln).then_inc(gate_exp, 1)
                c_copy(i, 0, 0)
                c_copy(i, 0, 1)
                round_ahead(n1)
                c_copy(i, 0, 2)
                c_copy(i, 0, 3)
                round_ahead(n1 + 1)
                c_tanh(i, [(0, 0), (0, 1), (0, 2)])
                act.wait_ge(cols_turned, 1)
                nc.scalar.activation(gc_col.rearrange("p c h -> p (c h)"), bank[2][:, 0:32], ACT.Copy).then_inc(cols_copied, 1)
                nc.scalar.activation(beta_col.rearrange("p c h -> p (c h)"), bank[3][:, 0:32], ACT.Copy).then_inc(cols_copied, 1)
                act.wait_ge(cols_copied, 2)
                nc.scalar.activation(beta_g, gc_col, ACT.Exp).then_inc(col_exp, 1)
                act.wait_ge(last_spread, 1)
                nc.scalar.activation(e_last.rearrange("p c h -> p (c h)"), bank[4][:, 0:32], ACT.Exp).then_inc(col_exp, 1)
                act.wait_ge(col_exp, 3)
                nc.scalar.activation(k_decay, k_decay, ACT.Exp).then_inc(col_exp, 1)
                for h in range(C_HEADS):
                    nxt = h + 1 < C_HEADS
                    if h:
                        act.wait_ge(osum_done, h)
                    for k in range(2):
                        act.wait_ge(silu_done, tanh_index(h, k) + 1)
                        nc.scalar.activation(csq[k], cy[h % 2][k], ACT.Square).then_inc(csq_done, 1)
                    for k in range(2):
                        act.wait_ge(csum_done, 2 * h + k + 1)
                        nc.scalar.activation(crs[k], bank[4 + k][:], ACT.Ln, bias=eps_col[:]).then_inc(cln_done, 1)
                    for k in range(2):
                        act.wait_ge(cln_done, 2 * h + k + 1)
                        nc.scalar.activation(crs[k], crs[k], ACT.Exp, scale=-0.5).then_inc(crs_done, 1)
                    act.wait_ge(rows_spread, h + 1)
                    nc.scalar.activation(grow, bk4(2), ACT.Exp).then_inc(grow_done, 1)
                    act.wait_ge(age_done, h + 1)
                    nc.scalar.activation(decay, decay, ACT.Exp).then_inc(decay_done, 1)
                    act.wait_ge(t_turned, h + 1)
                    nc.scalar.activation(Tm, bk4(2), ACT.Copy).then_inc(t_init, 1)
                    for k in range(1, LEVELS):
                        act.wait_ge(w_done, 6 * h + k)
                        nc.scalar.activation(Wm, bk4(3), ACT.Copy).then_inc(w_copied, 1)
                        if k == 1 and nxt:
                            c_copy(i, h + 1, 0)
                        if k == 4 and nxt:
                            c_copy(i, h + 1, 1)
                            round_ahead(n1 + 2 * h + 2)
                    act.wait_ge(wt_done, h + 1)
                    nc.scalar.activation(wt, bk4(4), ACT.Copy, scale=-1.0).then_inc(wt_copied, 1)
                    for c in range(NB):
                        act.wait_ge(vn_done, 4 * h + c + 1)
                        nc.scalar.activation(vn[c % 2], bk4(5)[:, c, :], ACT.Copy).then_inc(vn_copied, 1)
                        if c == 0 and nxt:
                            c_copy(i, h + 1, 2)
                    c_tanh(i, ([(h + 1, 0), (h + 1, 1), (h + 1, 2)] if nxt else []) + [(h, 3)])
                    act.wait_ge(o_done, h + 1)
                    nc.scalar.activation(csq[0], bank[2][:], ACT.Square).then_inc(osq_done, 1)
                    act.wait_ge(osum_done, h + 1)
                    nc.scalar.activation(ors, bank[3][:], ACT.Ln, bias=eps_col[:], scale=1.0 / P).then_inc(oln_done, 1)
                    act.wait_ge(oln_done, h + 1)
                    nc.scalar.activation(ors, ors, ACT.Exp, scale=-0.5).then_inc(ors_done, 1)
                    if nxt:
                        c_copy(i, h + 1, 3)
                        round_ahead(n1 + 2 * h + 3)
                    act.wait_ge(y32_done, h + 1)
                    nc.scalar.activation(g_hi[:, h, :], cyo, ACT.Copy).then_inc(yh_done, 1)

            act.preload_act_table_set("natural_log_exp_and_others")
            act.wait_ge(const_loaded, 80)
            nc.scalar.activation(par[:, G_AQ:G_AQ + 2], par[:, G_AQ:G_AQ + 2], ACT.Copy, scale=HD ** -0.5).then_inc(scaled, 1)
            nc.scalar.activation(par[:, G_BQ:G_BQ + 1], par[:, G_BQ:G_BQ + 1], ACT.Copy, scale=HD ** -0.5).then_inc(scaled, 1)
            nc.scalar.activation(par[:, G_CONV:NPARAM], par[:, G_CONV:NPARAM], ACT.Copy, scale=0.5).then_inc(scaled, 1)
            act.wait_ge(scaled, 4)
            act.wait_ge(bias_added, 1)
            nc.scalar.dma_start(bias_dram, bias_rows[0:BIAS_COLS, :]).then_inc(bias_saved, 16)
            for n in range(2):
                rounding(n, CHUNKS[n][3])
            for c in range(CT):
                square_x(0, c, 0)
            act.wait_ge(bias_saved, 16)
            for li, i in enumerate(layers):
                norm(2 * li)
                act.wait_ge(hl_done, 8 * (2 * li + 1))
                (mixer_a, mixer_b, mixer_c)[KINDS[i]](i)
                residual(first_chunk["out", i], added(li, False), 2 * li + 1, None)
                norm(2 * li + 1)
                mlp(li, i, 2 * li + 2 if li + 1 < len(layers) else None)

        @block.vector
        def _(dve):
            def sum_square(m, c):
                if c == 0:
                    return
                dve.wait_ge(sq_done, 8 * m + c + 1)
                if c >= 2:
                    dve.wait_ge(ss_added, 7 * m + c - 1)
                nc.vector.tensor_tensor(ss, sq[0] if c == 1 else ss, sq[c % 2], ALU.add).then_inc(ss_added, 1)

            def norm(m):
                gain = (G_MIX if m % 2 == 0 else G_MLP) + CT * layers[m // 2]
                dve.wait_ge(rs_done, m + 1)
                for c in range(CT + 1):
                    if c < CT:
                        if c >= 2:
                            dve.wait_ge(hl_done, 8 * m + c - 1)
                        nc.vector.scalar_tensor_tensor(h32[c % 2], x[:, c, :], par[:, gain + c:gain + c + 1], rs,
                                                       ALU.mult, ALU.mult).then_inc(h32_done, 1)
                    if c:
                        dve.wait_ge(hh_done, 8 * m + c)
                        nc.vector.tensor_tensor(h_lo[:, c - 1, :], h32[(c - 1) % 2], h_hi[:, c - 1, :].bitcast(F32),
                                                ALU.subtract).then_inc(hl_done, 1)

            def residual(t0, x0, m):
                for c in range(CT):
                    dve.wait_ge(lin_done, t0 + c + 1)
                    nc.vector.tensor_tensor(x[:, c, :], x[:, c, :], lin_bank[(t0 + c) % 2][:], ALU.add).then_inc(x_added, 1)
                    if m is not None:
                        sum_square(m, c)

            def hidden(lin_v, relu_v, g_v):
                for j in range(8):
                    dve.wait_ge(relu_done, relu_v[j + 1])
                    if j >= 2:
                        dve.wait_ge(gl_done, g_v[j - 1])
                    nc.vector.tensor_tensor(gsq[j % 2], relu_t[j % 2], relu_t[j % 2], ALU.mult).then_inc(gsq_done, 1)
                    dve.wait_ge(gh_done, g_v[j + 1])
                    nc.vector.tensor_tensor(g_lo[:, j, :], gsq[j % 2], g_hi[:, j, :].bitcast(F32),
                                            ALU.subtract).then_inc(gl_done, 1)

            def mlp(li, i, m):
                T, G, X = 2 * first_chunk["mlp", i], 8 * QUARTERS * li, added(li, True)
                with dve.Fori(0, QUARTERS - 1) as q:
                    g = {k: dve.snap(q * 8 + (G + k)) for k in range(1, 9)}
                    t = {c: dve.snap(q * 16 + (T + 8 + c + 1)) for c in range(CT)}
                    hidden(None, g, g)
                    for c in range(CT):
                        dve.wait_ge(lin_done, t[c])
                        nc.vector.tensor_tensor(x[:, c, :], x[:, c, :], lin_bank[c % 2][:], ALU.add).then_inc(x_added, 1)
                q = QUARTERS - 1
                g = {k: G + 8 * q + k for k in range(9)}
                hidden(None, g, g)
                residual(T + 16 * q + 8, X + 8 * q, m)

            def logits(u):
                k = u["u"] % 4
                prev = rank_in_ring(u)
                if prev is not None:
                    dve.wait_ge(pt_done, prev["t0"] + prev["tp"])
                off = 0
                for p, (g, ka, kz) in enumerate(u["pieces"]):
                    n = P * (kz - ka)
                    s = u["s0"] + p
                    if p == 0:
                        if u["kind"] == 1 and u["b"]:
                            dve.wait_ge(tm_done, u["tm"] + 1)
                        else:
                            dve.wait_ge(bias_loaded[u["H"] % 2], heads[u["H"]]["loaded"])
                    dve.wait_ge(s_done, s + 1)
                    nc.vector.tensor_tensor_reduce(out=l_of(u)[:, off:off + n], in0=bank[2 + s % 2][:, 0:n],
                                                   in1=bias_of(u, g, ka, kz), scale=1.0, scalar=TAKEN, op0=ALU.add,
                                                   op1=ALU.max, accum_out=mx[k][:, p:p + 1]).then_inc(l_done, 1)
                    off += n
                dve.wait_ge(l_done, u["s0"] + len(u["pieces"]))
                nc.vector.tensor_reduce(out=negmax[k], in_=mx[k][:, 0:len(u["pieces"])], op=ALU.max, axis=AX.X,
                                        negate=True).then_inc(negmax_done, 1)

            def copy_pieces(u):
                for p in range(u["tp"]):
                    n = P * min(4, len(u["blocks"]) - 4 * p)
                    t = u["t0"] + p
                    dve.wait_ge(pt_done, t + 1)
                    v = u["v0"] + p
                    if v >= 2:
                        dve.wait_ge(pv_done, v - 1)
                    nc.vector.tensor_copy(mem[u["kind"]]["pt"][v % 2][:, 0:n], bank[4 + t % 2][:, 0:n]).then_inc(pt_copied, 1)

            def outputs(u):
                k = u["u"] % 4
                dve.wait_ge(p_done, u["u"] + 1)
                nc.vector.reciprocal(rinv[k], psum_of[k]).then_inc(rinv_done, 1)
                dve.wait_ge(rinv_done, u["u"] + 1)
                dve.wait_ge(pv_done, u["v0"] + u["tp"])
                nc.vector.tensor_scalar(mem[u["kind"]]["y"][:, u["b"], HD * u["half"]:HD * u["half"] + HD],
                                        bank[6][:, 0:HD], rinv[k], None, ALU.mult).then_inc(y_done, 1)

            def y_low(h):
                dve.wait_ge(yh_done, h["y"] + 1)
                nc.vector.tensor_tensor(g_lo[:, h["f"], :], mem[h["kind"]]["yf"], g_hi[:, h["f"], :].bitcast(F32),
                                        ALU.subtract).then_inc(yl_done, 1)

            def y_copy(h):
                dve.wait_ge(pt_done, h["yt"] + 1)
                if h["y"]:
                    dve.wait_ge(yl_done, h["y"])
                nc.vector.tensor_copy(by_block(ayf), reversed_blocks(bank[4 + h["yt"] % 2][:])).then_inc(pt_copied, 1)

            def mixer_a(i):
                U = units_of(i)
                for f in range(A_PAIRS):
                    for k in range(8):
                        s = 8 * f + k
                        logits(U[s])
                        if k == 1 and f:
                            y_copy(pair_of(i, f - 1))
                        if k == 2 and f:
                            y_low(pair_of(i, f - 1))
                        if s:
                            copy_pieces(U[s - 1])
                            outputs(U[s - 1])
                copy_pieces(U[-1])
                outputs(U[-1])
                y_copy(pair_of(i, A_PAIRS - 1))
                y_low(pair_of(i, A_PAIRS - 1))

            def mixer_b(i):
                U = units_of(i)
                dve.wait_ge(iw_ready, 1)
                for p in range(24):
                    b, hd = 3 - p // 8, p % 8
                    n = P * (b + 1)
                    dve.wait_ge(idx_relu, p + 1)
                    w = bw[:, b, hd:hd + 1]
                    if hd == 0:
                        nc.vector.tensor_scalar(score[b], brelu[p % 2][:, 0:n], w, None, ALU.mult).then_inc(idx_acc, 1)
                    else:
                        dve.wait_ge(idx_acc, p)
                        nc.vector.scalar_tensor_tensor(score[b], brelu[p % 2][:, 0:n], w, score[b], ALU.mult,
                                                       ALU.add).then_inc(idx_acc, 1)
                step = 0
                dve.wait_ge(idx_acc, 24)
                for b in (3, 2, 1):
                    nc.vector.tensor_tensor(score[b][:, P * b:P * b + P], score[b][:, P * b:P * b + P], causal,
                                            ALU.add).then_inc(topk_step, 1)
                    step += 1
                    for _ in range(TOPK // 8):
                        dve.wait_ge(topk_step, step)
                        nc.vector.max(best, score[b]).then_inc(topk_step, 1)
                        dve.wait_ge(topk_step, step + 1)
                        nc.vector.match_replace(out=score[b], in_to_replace=best, in_values=score[b],
                                                imm_value=TAKEN).then_inc(topk_step, 1)
                        step += 2
                    dve.wait_ge(topk_step, step)
                    nc.vector.tensor_scalar(score[b], score[b], TAKEN / 1.5, MASKED, ALU.is_gt,
                                            ALU.mult).then_inc(mask_ready, 1)
                for s in range(len(U) + SKEW[1]):
                    if s < len(U):
                        logits(U[s])
                    if s >= SKEW[1]:
                        if (s - SKEW[1]) % 8 == 1 and s > SKEW[1] + 1:
                            y_low(pair_of(i, (s - SKEW[1]) // 8 - 1))
                        outputs(U[s - SKEW[1]])
                y_low(pair_of(i, 7))

            def conv_steps(i, h, k, steps):
                t = 3 * h + k
                y, xt = cy[h % 2][k], cx[t % 2]
                for s in steps:
                    w = par[:, G_CONV + (3 - s) * 3 * C_HEADS + k * C_HEADS + h:][:, 0:1]
                    if s == 0:
                        dve.wait_ge(copied, copy_first[i] + 2 + 4 * h + k + 1)
                        nc.vector.tensor_scalar(y, xt, w, None, ALU.mult).then_inc(conv_step, 1)
                    else:
                        dve.wait_ge(conv_step, 3 * t + s)
                        nc.vector.scalar_tensor_tensor(y[:, s:], xt[:, :TOK - s], w, y[:, s:], ALU.mult,
                                                       ALU.add).then_inc(conv_step if s < 3 else conv_done, 1)

            def silu(h, k):
                n = tanh_index(h, k)
                dve.wait_ge(tanh_done, n + 1)
                y = cy[h % 2][k] if k < 3 else cg[h % 2]
                nc.vector.scalar_tensor_tensor(y, cth[n % 2], 1.0, y, ALU.add, ALU.mult).then_inc(silu_done, 1)

            def c_gates_steps(i):
                step = [0]
                C8 = slice(0, C_HEADS)

                def link(ins):
                    step[0] += 1
                    ins.then_inc(gate_step, 1)
                    dve.wait_ge(gate_step, step[0])

                dve.wait_ge(copied, copy_first[i] + 1)
                link(nc.vector.tensor_scalar(beta_row[C8, :], beta_row[C8, :], 1.0, 0.5, ALU.add, ALU.mult))
                nc.vector.tensor_copy(head_sel[C8], ident[C8, 0:C_HEADS].unsqueeze(2).to_broadcast([C_HEADS, C_HEADS, P]))
                dve.wait_ge(gate_exp, 3)
                nc.vector.tensor_scalar(gu, ge, 1.0, None, ALU.add).then_inc(gate_ln, 1)
                dve.wait_ge(gate_ln, 1)
                link(nc.vector.tensor_scalar(gd, gu, 1.0, None, ALU.subtract))
                link(nc.vector.tensor_scalar(gr, gd, 1e-30, None, ALU.max))
                link(nc.vector.reciprocal(gr, gr))
                link(nc.vector.tensor_tensor(gr, gr, ge, ALU.mult))
                dve.wait_ge(gate_exp, 4)
                link(nc.vector.tensor_tensor(gr, gr, gl_, ALU.mult))
                link(nc.vector.scalar_tensor_tensor(gd, gd, 0.0, ge, ALU.is_equal, ALU.mult))
                link(nc.vector.tensor_tensor(gr, gr, gd, ALU.add))
                link(nc.vector.scalar_tensor_tensor(gr, gz, 0.0, gr, ALU.max, ALU.add))
                link(nc.vector.tensor_scalar(gr, gr, neg_a[C8, :], -1.0, ALU.mult, ALU.mult))
                for c in range(NB):
                    ins = nc.vector.tensor_tensor_scan(gc_row[C8, P * c:P * c + P], ones[C8, :], gr[:, P * c:P * c + P],
                                                       0.0, ALU.mult, ALU.add)
                ins.then_inc(gates_ready, 1)

            def mixer_c(i):
                c_gates_steps(i)
                for k in range(3):
                    conv_steps(i, 0, k, range(4))
                for k in range(3):
                    silu(0, k)
                dve.wait_ge(col_exp, 1)
                nc.vector.tensor_tensor(beta_g, beta_g, beta_col, ALU.mult)
                dve.wait_ge(last_spread, 1)
                dve.wait_ge(col_exp, 2)
                nc.vector.tensor_tensor(k_decay, bank[4][:, 0:32].rearrange("p (c h) -> p c h", c=NB), gc_col,
                                        ALU.subtract).then_inc(col_exp, 1)
                for h in range(C_HEADS):
                    nxt = h + 1 < C_HEADS

                    def spread(col):
                        return col[:, :, h:h + 1].to_broadcast([P, NB, P])

                    dve.wait_ge(crs_done, 2 * h + 2)
                    f = lambda m: m.rearrange("p c n -> p (c n)")
                    nc.vector.scalar_tensor_tensor(f(qn), cy[h % 2][0], float(P) ** -0.5, crs[0], ALU.mult, ALU.mult)
                    nc.vector.tensor_tensor(f(kn), cy[h % 2][1], crs[1], ALU.mult).then_inc(qkn_done, 1)
                    dve.wait_ge(grow_done, h + 1)
                    for c in range(NB):
                        ins = nc.vector.scalar_tensor_tensor(decay[:, c, :], bk4(2)[:, c, :], gc_col[:, c, h:h + 1],
                                                             m_decay, ALU.subtract, ALU.add)
                    ins.then_inc(age_done, 1)
                    dve.wait_ge(qkn_done, h + 1)
                    nc.vector.tensor_tensor(qe, qn, grow, ALU.mult).then_inc(qe_done, 1)
                    dve.wait_ge(kk_done, h + 1)
                    dve.wait_ge(decay_done, h + 1)
                    nc.vector.tensor_tensor(at, bk4(6), decay, ALU.mult).then_inc(at_raw, 1)
                    nc.vector.tensor_tensor(qkd, bk4(7), decay, ALU.mult)
                    dve.wait_ge(at_raw, h + 1)
                    nc.vector.tensor_tensor(at, at, bk4(3), ALU.mult).then_inc(at_done, 1)
                    dve.wait_ge(kv_turned, h + 1)
                    nc.vector.tensor_tensor(v_beta, bk4(5), spread(beta_col), ALU.mult)
                    nc.vector.tensor_tensor(k_beta, bk4(4), spread(beta_g), ALU.mult)
                    if h == 0:
                        dve.wait_ge(col_exp, 4)
                    nc.vector.tensor_tensor(k_dec, bk4(4), spread(k_decay), ALU.mult).then_inc(kv_scaled, 1)
                    dve.wait_ge(atl_done, 7 * h + 1)
                    nc.vector.tensor_tensor(Um, ident.unsqueeze(1).to_broadcast([P, NB, P]), atl[0],
                                            ALU.subtract).then_inc(u_done, 1)
                    for k in range(1, LEVELS):
                        dve.wait_ge(tw_done, 6 * h + k)
                        if k < LEVELS - 1:
                            a = halves_of(Tm, k, False)
                            nc.vector.tensor_tensor(a, a, packed(6, k), ALU.subtract).then_inc(t_done, 1)
                        a = halves_of(Um, k, True)
                        nc.vector.tensor_tensor(a, a, packed(7, k), ALU.subtract).then_inc(u_done, 1)
                        if nxt and k in (2, 3, 5, 6):
                            conv_steps(i, h + 1, k // 4, (0, 1) if k in (2, 5) else (2, 3))
                    for c in range(NB - 1):
                        dve.wait_ge(ds_done, 3 * h + c + 1)
                        src = bank[6 + c % 2][:, 0:P]
                        if c == 0:
                            nc.vector.tensor_copy(state, src).then_inc(state_done, 1)
                        else:
                            nc.vector.scalar_tensor_tensor(state, state, e_last[:, c, h:h + 1], src, ALU.mult,
                                                           ALU.add).then_inc(state_done, 1)
                            if nxt:
                                conv_steps(i, h + 1, 2, (0, 1) if c == 1 else (2, 3))
                    for k in range(3):
                        if nxt:
                            silu(h + 1, k)
                    silu(h, 3)
                    dve.wait_ge(ors_done, h + 1)
                    nc.vector.scalar_tensor_tensor(on, bank[2][:], par[:, G_CO:G_CO + 1], ors, ALU.mult,
                                                   ALU.mult).then_inc(on_done, 1)
                    dve.wait_ge(on_done, h + 1)
                    dve.wait_ge(silu_done, tanh_index(h, 3) + 1)
                    nc.vector.tensor_tensor(cyo, on, cg[h % 2], ALU.mult).then_inc(y32_done, 1)
                    dve.wait_ge(yh_done, y_first[i] + h + 1)
                    nc.vector.tensor_tensor(g_lo[:, h, :], cyo, g_hi[:, h, :].bitcast(F32), ALU.subtract).then_inc(yl_done, 1)

            dve.wait_ge(bias_mm, 1)
            nc.vector.tensor_tensor(bias_rows[0:BIAS_COLS, 0:TOK], bank[2][0:BIAS_COLS, :], bmask_sb[0:BIAS_COLS, 0:TOK],
                                    ALU.add)
            nc.vector.tensor_tensor(bias_rows[0:BIAS_COLS, TOK:RW], bank[3][0:BIAS_COLS, 0:P],
                                    bmask_sb[0:BIAS_COLS, TOK:RW], ALU.add).then_inc(bias_added, 1)
            for c in range(CT):
                dve.wait_ge(x_turned, c + 1)
                nc.vector.tensor_copy(x[:, c, :], bank[4 + c % 2][:]).then_inc(x_added, 1)
                sum_square(0, c)
            for li, i in enumerate(layers):
                norm(2 * li)
                (mixer_a, mixer_b, mixer_c)[KINDS[i]](i)
                residual(2 * first_chunk["out", i], added(li, False), 2 * li + 1)
                norm(2 * li + 1)
                mlp(li, i, 2 * li + 2 if li + 1 < len(layers) else None)
            for b in range(NB):
                for half in range(2):
                    k = 2 * b + half
                    dve.wait_ge(out_turned, k + 1)
                    nc.vector.tensor_copy(x_tok[:, b, half * 512:half * 512 + 512], bank[4 + k % 2][:]).then_inc(out_copied, 1)

        @block.tensor
        def _(pe):
            def product(n, t, acts, kt, lo, hi, act_sem, act0, tok):
                s, j = n % 2, t % 2
                b = lin_bank[t % 2]
                a_hi, a_lo = acts
                steps = []
                if not tok:
                    cols = slice(P * j, P * j + P)
                    for c in range(kt):
                        for w, a in ((w_hi, a_hi), (w_hi, a_lo), (w_lo, a_hi)):
                            steps.append((b[:], w[s][:, c, cols], a[:, c, :], c, len(steps) == 0, len(steps) == 3 * kt - 1))
                else:
                    for tb in (2 * j, 2 * j + 1):
                        for c in range(kt):
                            for z, (w, a) in enumerate(((w_hi, a_hi), (w_hi, a_lo), (w_lo, a_hi))):
                                steps.append((b[:, CW * (tb % 2):CW * (tb % 2) + CW], a[:, c, P * tb:P * tb + P],
                                              w[s][:, c, :], c, c + z == 0, c == kt - 1 and z == 2))
                lo, hi = lo * len(steps) // 24, hi * len(steps) // 24
                if lo == 0:
                    pe.wait_ge(w_lo_done, n + 1)
                    if t >= 2 and evac[t - 2][0] is not None:
                        pe.wait_ge(*evac[t - 2])
                for k in range(lo, hi):
                    o, lhsT, rhs, c, start, stop = steps[k]
                    if act_sem is not None and (k == 0 or steps[k - 1][3] < c) :
                        pe.wait_ge(act_sem, act0 + c + 1)
                    mm = nc.tensor.matmul(o, lhsT, rhs, start=start, stop=stop)
                if hi == len(steps):
                    mm.then_inc(lin_done, 1)

            H = (h_hi, h_lo)

            def norm(m):
                pe.wait_ge(ss_added, 7 * (m + 1))
                nc.tensor.matmul(stat_bank[:], ones, ss, start=True, stop=True).then_inc(norm_sum, 1)

            def out_proj(li, i):
                n0, kt = first_chunk["out", i], CHUNKS[first_chunk["out", i]][3]
                y0 = y_first[i]
                for k in range(4):
                    for j in range(2):
                        t = 2 * (n0 + k) + j
                        product(n0 + k, t, (g_hi, g_lo), kt, 0, 24, yl_done, y0, None)

            def mlp_quarter(n, v_lo, v_x, v_relu, v_g):
                for k in range(8):
                    s = (n + k) % 2
                    for j in range(2):
                        t = 2 * k + j
                        if j == 0:
                            pe.wait_ge(w_lo_done, v_lo[k])
                        if t < 2:
                            pe.wait_ge(x_added, v_x[t - 1])
                        elif t < 10:
                            pe.wait_ge(relu_done, v_relu[t - 1])
                        else:
                            pe.wait_ge(x_added, v_x[t - 9])
                        a_hi, a_lo = (h_hi, h_lo) if k < 4 else (g_hi, g_lo)
                        for c in range(CT):
                            if k == 4 and j == 0:
                                pe.wait_ge(gl_done, v_g[c + 1])
                            for z, (w, a) in enumerate(((w_hi, a_hi), (w_hi, a_lo), (w_lo, a_hi))):
                                mm = nc.tensor.matmul(lin_bank[j][:], w[s][:, c, P * j:P * j + P], a[:, c, :],
                                                      start=c + z == 0, stop=c == CT - 1 and z == 2)
                        mm.then_inc(lin_done, 1)

            def mlp(li, i):
                n = first_chunk["mlp", i]
                G, X = 8 * QUARTERS * li, added(li, True)
                pe.wait_ge(hl_done, 8 * (2 * li + 2))
                with pe.Fori(0, QUARTERS) as q:
                    v_lo = [pe.snap(q * 8 + (n + k + 1)) for k in range(8)]
                    v_x = {k: pe.snap(q * 8 + (X + k)) for k in range(-1, 7)}
                    v_g = {k: pe.snap(q * 8 + (G + k)) for k in range(1, 9)}
                    mlp_quarter(n, v_lo, v_x, v_g, v_g)

            def scores(u):
                for p, (g, ka, kz) in enumerate(u["pieces"]):
                    s = u["s0"] + p
                    q, k = qk_of(u, g)
                    if u["kind"] == 0:
                        pe.wait_ge(qk_ready, q_first[u["i"]] + 6 * u["f"] + 2 * g + 2)
                    if s >= 2:
                        pe.wait_ge(l_done, s - 1)
                    b = u["b"]
                    nc.tensor.matmul(bank[2 + s % 2][:, 0:P * (kz - ka)], q[:, P * b:P * b + P], k[:, P * ka:P * kz],
                                     start=True, stop=True).then_inc(s_done, 1)

            def turn(u, p):
                t = u["t0"] + p
                nb = min(4, len(u["blocks"]) - 4 * p)
                if p == 0:
                    pe.wait_ge(p_done, u["u"] + 1)
                if t >= 2:
                    pe.wait_ge(pt_copied, t - 1)
                for k in range(nb):
                    c = P * (4 * p + k)
                    mm = nc.tensor.transpose(bank[4 + t % 2][:, P * k:P * k + P], l_of(u)[:, c:c + P], ident)
                mm.then_inc(pt_done, 1)

            def weigh(u, p):
                t = u["t0"] + p
                pe.wait_ge(pt_copied, t + 1)
                if p == 0 and u["u"]:
                    pe.wait_ge(y_done, u["u"])
                nb = len(u["blocks"])
                for k in range(4 * p, min(4 * p + 4, nb)):
                    g, kb = u["blocks"][k]
                    mm = nc.tensor.matmul(bank[6][:, 0:HD], mem[u["kind"]]["pt"][(u["v0"] + p) % 2][:, P * (k % 4):P * (k % 4) + P],
                                          v_of(u, g, kb), start=k == 0, stop=k == nb - 1)
                mm.then_inc(pv_done, 1)

            def attend(u):
                turn(u, 0)
                for p in range(1, u["tp"]):
                    turn(u, p)
                    weigh(u, p - 1)
                weigh(u, u["tp"] - 1)

            def turn_outputs(h):
                pe.wait_ge(y_done, h["ylast"])
                pe.wait_ge(pt_copied, h["yt"] - 1)
                y = mem[h["kind"]]["y"]
                for b in range(NB):
                    mm = nc.tensor.transpose(bank[4 + h["yt"] % 2][:, P * b:P * b + P], y[:, b, :], ident)
                mm.then_inc(pt_done, 1)

            def sum_qk(kind, Q):
                pe.wait_ge(qsq_done, Q + 1)
                if Q:
                    pe.wait_ge(qln_done, Q)
                nc.tensor.matmul(stat_bank[:], halves, mem[kind]["sq"], start=True, stop=True).then_inc(ssq_done, 1)

            def mixer_a(li, i):
                n0, n1, Q, U = first_chunk["av", i], first_chunk["aqk", i], q_first[i], units_of(i)
                for v in range(6):
                    for j in range(2):
                        product(n0 + v, 2 * (n0 + v) + j, H, CT, 0, 24, hl_done if v == 0 else None, 16 * li, "pair")

                def tile(n, k, Q):
                    product(n + k // 2, 2 * n + k, H, CT, 0, 12, None, 0, None)
                    if k:
                        sum_qk(0, Q + k - 1)
                    product(n + k // 2, 2 * n + k, H, CT, 12, 24, None, 0, None)

                for k in range(6):
                    tile(n1, k, Q)
                sum_qk(0, Q + 5)
                pe.wait_ge(copied, copy_first[i] + 12)
                for f in range(A_PAIRS):
                    Q1, n2 = Q + 6 * (f + 1), n1 + 3 * (f + 1)
                    more = f + 1 < A_PAIRS
                    for k in range(8):
                        s = 8 * f + k
                        scores(U[s])
                        if k == 1 and f:
                            turn_outputs(pair_of(i, f - 1))
                        if more and k < 6:
                            tile(n2, k, Q1)
                        if more and k == 6:
                            sum_qk(0, Q1 + 5)
                        if s:
                            attend(U[s - 1])
                attend(U[-1])
                turn_outputs(pair_of(i, A_PAIRS - 1))

            def mixer_b(li, i):
                n0, Q, U = first_chunk["bkw", i], q_first[i], units_of(i)
                t0 = 2 * n0
                product(n0, t0, H, CT, 0, 24, hl_done, 16 * li, None)
                product(n0, t0 + 1, H, CT, 0, 24, None, 0, None)
                for k in range(4):
                    product(n0 + 1 + k // 2, t0 + 2 + k, H, CT, 0, 24, None, 0, None)
                    if k == 0:
                        pe.wait_ge(copied, copy_first[i] + 2)
                        for b in range(NB):
                            mm = nc.tensor.transpose(bank[4][:, B_IDX * b:B_IDX * b + B_IDX],
                                                     bw_row[0:B_IDX, P * b:P * b + P], ident[0:B_IDX, 0:B_IDX])
                        mm.then_inc(iw_turned, 1)
                pe.wait_ge(copied, copy_first[i] + 6)
                for k in range(12):
                    t, n = t0 + 6 + k, n0 + 3 + k // 2
                    for z in range(4):
                        if k < 6:
                            p = 4 * k + z
                            b, hd = 3 - p // 8, p % 8
                            if p >= 2:
                                pe.wait_ge(idx_relu, p - 1)
                            r = slice(HD * (hd % 2), HD * (hd % 2) + HD)
                            nc.tensor.matmul(bank[2 + p % 2][:, 0:P * (b + 1)], bqi[hd // 2][r, P * b:P * b + P],
                                             bki[r, 0:P * (b + 1)], start=True, stop=True).then_inc(idx_done, 1)
                        if z == 2 and k >= 3:
                            sum_qk(1, Q + k - 3)
                        product(n, t, H, CT, 6 * z, 6 * z + 6, None, 0, "pair" if k < 2 else None)
                sum_qk(1, Q + 9)
                pe.wait_ge(qk_ready, Q + 10)
                pe.wait_ge(idx_relu, 24)
                for s in range(len(U) + SKEW[1]):
                    if s < len(U):
                        scores(U[s])
                    if s >= SKEW[1]:
                        if (s - SKEW[1]) % 8 == 0 and s > SKEW[1]:
                            turn_outputs(pair_of(i, (s - SKEW[1]) // 8 - 1))
                        attend(U[s - SKEW[1]])
                turn_outputs(pair_of(i, 7))

            def mixer_c(li, i):
                n0, n1 = first_chunk["cab", i], first_chunk["chd", i]
                C8 = slice(0, C_HEADS)
                product(n0, 2 * n0, H, CT, 0, 24, hl_done, 16 * li, None)
                product(n0, 2 * n0 + 1, H, CT, 0, 24, None, 0, None)

                def fill(h, lo, hi):
                    if h < C_HEADS:
                        for k in range(4):
                            a, z = max(lo, 24 * k), min(hi, 24 * k + 24)
                            if a < z:
                                product(n1 + 2 * h + k // 2, 2 * n1 + 4 * h + k, H, CT, a - 24 * k, z - 24 * k, None, 0, None)

                fill(0, 0, 96)
                pe.wait_ge(gates_ready, 1)
                for k, rows in enumerate((gc_row, beta_row)):
                    for c in range(NB):
                        mm = nc.tensor.transpose(bank[2 + k][:, C_HEADS * c:C_HEADS * c + C_HEADS],
                                                 rows[C8, P * c:P * c + P], ident[C8, C8])
                mm.then_inc(cols_turned, 1)
                pe.wait_ge(cols_copied, 2)
                pe.wait_ge(cmask_loaded, 32)
                nc.tensor.matmul(bank[4][:, 0:32], m_last, gc_col.rearrange("p c h -> p (c h)"), start=True,
                                 stop=True).then_inc(last_spread, 1)
                for h in range(C_HEADS):
                    at_ = [0]

                    def filler(to):
                        fill(h + 1, at_[0], to)
                        at_[0] = to

                    for k in range(2):
                        pe.wait_ge(csq_done, 2 * h + k + 1)
                        if k == 0:
                            pe.wait_ge(col_exp, 3) if h == 0 else pe.wait_ge(wt_copied, h)
                        elif h:
                            pe.wait_ge(vn_copied, 4 * h)
                        nc.tensor.matmul(bank[4 + k][:], ones, csq[k], start=True, stop=True).then_inc(csum_done, 1)
                    if h:
                        pe.wait_ge(on_done, h)
                    nc.tensor.matmul(bank[2][:], head_sel[C8, h, :], gc_row[C8, :], start=True, stop=True)
                    nc.tensor.matmul(bank[3][:], head_sel[C8, h, :], beta_row[C8, :], start=True,
                                     stop=True).then_inc(rows_spread, 1)
                    filler(FILL["sums"])
                    pe.wait_ge(qkn_done, h + 1)
                    for c in range(NB):
                        nc.tensor.matmul(bk4(6)[:, c, :], kn[:, c, :], kn[:, c, :], start=True, stop=True)
                    for c in range(NB):
                        mm = nc.tensor.matmul(bk4(7)[:, c, :], kn[:, c, :], qn[:, c, :], start=True, stop=True)
                    mm.then_inc(kk_done, 1)
                    for c in range(NB):
                        nc.tensor.transpose(bk4(4)[:, c, :], kn[:, c, :], ident)
                    for c in range(NB):
                        mm = nc.tensor.transpose(bk4(5)[:, c, :], cy[h % 2][2][:, P * c:P * c + P], ident)
                    mm.then_inc(kv_turned, 1)
                    filler(FILL["products"])
                    pe.wait_ge(u_done, 7 * h + 1)
                    for c in range(NB):
                        mm = nc.tensor.transpose(bk4(2)[:, c, :], Um[:, c, :], ident)
                    mm.then_inc(t_turned, 1)
                    filler(FILL["t"])
                    for k in range(1, LEVELS):
                        if k == 1:
                            pe.wait_ge(t_init, h + 1)
                        else:
                            pe.wait_ge(t_done, 5 * h + k - 1)
                        pe.wait_ge(atl_done, 7 * h + k + 1)
                        for c in range(NB):
                            mm = nc.tensor.matmul(bk4(3)[:, c, :], atl[k % 3][:, c, :], Tm[:, c, :], start=True, stop=True)
                        mm.then_inc(w_done, 1)
                        filler(FILL_W[k])
                        pe.wait_ge(w_copied, 6 * h + k)
                        pe.wait_ge(u_done, 7 * h + k)
                        for c in range(NB):
                            if k < LEVELS - 1:
                                nc.tensor.matmul(packed(6, k)[:, c], Um[:, c, :], halves_of(Wm, k, False)[:, c],
                                                 start=True, stop=True)
                        for c in range(NB):
                            mm = nc.tensor.matmul(packed(7, k)[:, c], Wm[:, c, :], halves_of(Um, k, True)[:, c],
                                                  start=True, stop=True)
                        mm.then_inc(tw_done, 1)
                        filler(FILL_TW[k])
                    pe.wait_ge(u_done, 7 * h + 7)
                    pe.wait_ge(kv_scaled, h + 1)
                    for c in range(NB):
                        mm = nc.tensor.matmul(bk4(4)[:, c, :], k_beta[:, c, :], Um[:, c, :], start=True, stop=True)
                    mm.then_inc(wt_done, 1)
                    filler(FILL["wt"])
                    for c in range(NB):
                        mm = nc.tensor.matmul(bk4(5)[:, c, :], Um[:, c, :], v_beta[:, c, :], start=True, stop=c == 0)
                        if c:
                            if c == 1:
                                pe.wait_ge(wt_copied, h + 1)
                            pe.wait_ge(state_done, 3 * h + c)
                            mm = nc.tensor.matmul(bk4(5)[:, c, :], wt[:, c, :], state, start=False, stop=True)
                        mm.then_inc(vn_done, 1)
                        if c:
                            nc.tensor.matmul(bk4(2)[:, c, :], state, qe[:, c, :], start=True, stop=False)
                        filler(FILL["vn"][c])
                        pe.wait_ge(vn_copied, 4 * h + c + 1)
                        mm = nc.tensor.matmul(bk4(2)[:, c, :], vn[c % 2], qkd[:, c, :], start=c == 0, stop=True)
                        if c == NB - 1:
                            mm.then_inc(o_done, 1)
                        else:
                            nc.tensor.matmul(bank[6 + c % 2][:, 0:P], k_dec[:, c, :], vn[c % 2], start=True,
                                             stop=True).then_inc(ds_done, 1)
                        filler(FILL["ds"][c])
                    pe.wait_ge(osq_done, h + 1)
                    nc.tensor.matmul(bank[3][:], ones, csq[0], start=True, stop=True).then_inc(osum_done, 1)
                    filler(FILL["osum"])

            pe.wait_ge(const_loaded, 80)
            for k, (a, z) in enumerate(((0, TOK), (TOK, RW))):
                mm = nc.tensor.matmul(bank[2 + k][0:BIAS_COLS, 0:z - a], rb_in[0:BUCKETS, :], bucket_sb[0:BUCKETS, a:z],
                                      start=True, stop=True)
            mm.then_inc(bias_mm, 1)
            pe.wait_ge(x_loaded, 16 * NB)
            for c in range(CT):
                if c >= 2:
                    pe.wait_ge(x_added, c - 1)
                for b in range(NB):
                    mm = nc.tensor.transpose(bank[4 + c % 2][:, P * b:P * b + P], x_tok[:, b, P * c:P * c + P], ident)
                mm.then_inc(x_turned, 1)
            for li, i in enumerate(layers):
                norm(2 * li)
                (mixer_a, mixer_b, mixer_c)[KINDS[i]](li, i)
                out_proj(li, i)
                norm(2 * li + 1)
                mlp(li, i)
            pe.wait_ge(x_added, added(len(layers), False))
            for b in range(NB):
                for half in range(2):
                    k = 2 * b + half
                    if k >= 2:
                        pe.wait_ge(out_copied, k - 1)
                    for c in range(4):
                        mm = nc.tensor.transpose(bank[4 + k % 2][:, P * c:P * c + P],
                                                 x[:, 4 * half + c, P * b:P * b + P], ident)
                    mm.then_inc(out_turned, 1)


def t5_bucket(dist):
    exact = BUCKETS // 2
    d = np.maximum(dist, 1).astype(np.float32)
    part = np.log(d / np.float32(exact)) / np.float32(math.log(2048 / exact)) * np.float32(BUCKETS - exact)
    large = np.minimum(exact + part.astype(np.int32), BUCKETS - 1)
    return np.where(dist < exact, dist, large)


def constants():
    r, c = np.arange(P)[:, None], np.arange(P)[None, :]
    masks = np.zeros((NMASK, P, P), np.float32)
    masks[M_ID] = r == c
    masks[M_ONES] = 1.0
    masks[M_HALVES] = r // HD == c // HD
    masks[M_CAUSAL] = np.where(c > P - 1 - r, MASKED, 0.0)
    masks[M_DECAY] = np.where(r > c, MASKED, 0.0)
    masks[M_LAST] = (r == P - 1) * np.ones((1, P))
    for k in range(LEVELS):
        s = 1 << k
        masks[M_LEVEL + k] = (r // (2 * s) == c // (2 * s)) & (r % (2 * s) < s) & (c % (2 * s) >= s)
    dist = TOK - 1 - np.arange(RW)
    rows = np.zeros((BUCKETS, RW), np.float32)
    rows[t5_bucket(np.maximum(dist, 0)), np.arange(RW)] = dist >= 0
    mask = np.zeros((BIAS_COLS, RW), np.float32)
    for g, (window, dilation) in enumerate(A_GROUPS):
        ok = (dist >= 0) & (dist <= window) & (dist % dilation == 0)
        mask[g * A_HEADS:(g + 1) * A_HEADS] = np.where(ok, 0.0, MASKED)
    mask[len(A_GROUPS) * A_HEADS:] = np.where(dist >= 0, 0.0, MASKED)
    return masks.reshape(NMASK * P, P), rows, mask


def columns(v, times=1):
    v = np.asarray(v)
    return np.concatenate([v.reshape(-1, v.shape[-1])] * times, axis=1).reshape(-1, P).T


def layout(inputs):
    masks, bucket_rows, bias_mask = constants()
    params = np.concatenate([
        columns(inputs["norm_mix"]), columns(inputs["norm_mlp"]),
        columns(inputs["a_q_gain"], 2), columns(inputs["a_k_gain"], 2),
        columns(inputs["b_q_gain"], 2), columns(inputs["b_k_gain"], 2),
        columns(inputs["c_o_gain"]), columns(inputs["c_conv_w"]),
    ], axis=1)
    gates = np.concatenate([np.asarray(inputs["c_a_log"]).T, np.asarray(inputs["c_dt_bias"]).T], axis=1)
    arrays = {
        "x_in": np.asarray(inputs["x"])[0], "rel_bias": inputs["rel_bias"], "params": params, "c_gates": gates,
        "masks": masks, "bucket_rows": bucket_rows, "bias_mask": bias_mask,
    }
    for name in ("mlp_w1", "mlp_w2", "a_w_in", "a_w_out", "b_w_in", "b_w_out", "c_w_in", "c_w_out"):
        arrays[name] = inputs[name]
    return {k: np.ascontiguousarray(v) for k, v in arrays.items()}


def kernel(**inputs):
    import concourse.bacc as bacc
    from concourse.bass_utils import run_bass_kernel_spmd

    nc = bacc.Bacc("TRN2", target_bir_lowering=False, num_devices=1, dynamic_dma_scratch_size=1024)
    arrays = layout(inputs)
    aps = {k: nc.dram_tensor(f"in_{k}", v.shape, mybir.dt.from_np(v.dtype), kind="ExternalInput").ap()
           for k, v in arrays.items()}
    out = nc.dram_tensor("out_y", (TOK, DM), F32, kind="ExternalOutput").ap()
    trunk(nc, out=out, **aps)
    r = run_bass_kernel_spmd(nc, [{f"in_{k}": v for k, v in arrays.items()}], core_ids=[0])
    return r.results[0]["out_y"].reshape(1, TOK, DM)
```

```python
import math
from contextlib import ExitStack

import concourse.bass as bass
import numpy as np
from concourse import mybir

F32 = mybir.dt.float32
F32R = mybir.dt.float32r
ALU = mybir.AluOpType
ACT = mybir.ActivationFunctionType
AX = mybir.AxisListType

P = 128
TOK = 512
NB = TOK // P
DM = 1024
CT = DM // P
DEPTH = 4
FF = 4 * DM
QUARTERS = FF // DM
CW = 256
EPS = 1e-6
HD = 64
A_HEADS, A_GROUPS = 8, ((128, 1), (512, 4), (2048, 16))
A_PAIRS = A_HEADS // 2
B_HEADS, B_KV, B_IDX = 16, 4, 8
TOPK = 128
C_HEADS = 8
BUCKETS = 32
BIAS_COLS = len(A_GROUPS) * A_HEADS + B_HEADS
MASKED = -1.0e30
TAKEN = -3.0e38
RW = TOK + P
A_BIAS = (256, 512, 512)

G_MIX, G_MLP = 0, DEPTH * CT
G_AQ = 2 * DEPTH * CT
G_AK = G_AQ + 2
G_BQ = G_AK + 2
G_BK = G_BQ + 1
G_CO = G_BK + 1
G_CONV = G_CO + 1
NPARAM = G_CONV + 4 * 3 * C_HEADS
M_ID, M_ONES, M_HALVES = 0, 1, 2
M_CAUSAL, M_DECAY, M_LAST, M_LEVEL = 3, 4, 5, 6
LEVELS = 7
NMASK = M_LEVEL + LEVELS
COMMON_MASKS = 4

KINDS = (0, 1, 2, 0)


def plan():
    chunks = []
    for i in range(DEPTH):
        kind = KINDS[i]
        if kind == 0:
            chunks += [("av", i, v, CT, 1) for v in range(6)]
            chunks += [("aqk", i, c, CT, 2) for c in range(3 * A_PAIRS)]
            chunks += [("out", i, k, 4, 1) for k in range(4)]
        elif kind == 1:
            chunks += [("bkw", i, 0, CT, 4), ("bqi", i, 0, CT, 1), ("bqi", i, 1, CT, 1), ("bv", i, 0, CT, 1)]
            chunks += [("bq", i, c, CT, 4) for c in range(4)] + [("bk", i, 0, CT, 1)]
            chunks += [("out", i, k, CT, 4) for k in range(4)]
        else:
            chunks += [("cab", i, 0, CT, 4)]
            chunks += [("chd", i, c, CT, 2) for c in range(2 * C_HEADS)]
            chunks += [("out", i, k, CT, 1) for k in range(4)]
        chunks += [("mlp", i, c, CT, 1) for c in range(8 * QUARTERS)]
    return chunks


def trunk(nc, x_in, rel_bias, params, c_gates, masks, bucket_rows, bias_mask, mlp_w1, mlp_w2,
          a_w_in, a_w_out, b_w_in, b_w_out, c_w_in, c_w_out, out, layers=range(DEPTH)):
    CHUNKS = [c for c in plan() if c[1] in layers]
    N = len(CHUNKS)
    first_chunk = {}
    for n, c in enumerate(CHUNKS):
        first_chunk.setdefault(c[:2], n)

    raw_value, at = [], [0, 0]
    for n, c in enumerate(CHUNKS):
        at[n % 2] += 16 * c[4]
        raw_value.append(at[n % 2])

    def added(li, mlp):
        return CT * (1 + li * (1 + QUARTERS) + (1 if mlp else 0))

    with ExitStack() as ctx:
        def sb(name, shape, dt=F32):
            return ctx.enter_context(nc.sbuf_tensor(name, shape, dt))

        def sem(name):
            return ctx.enter_context(nc.semaphore(name))

        x = sb("x", [P, CT, TOK])
        h_hi, h_lo = sb("h_hi", [P, CT, TOK], F32R), sb("h_lo", [P, CT, TOK], F32R)
        g_hi, g_lo = sb("g_hi", [P, CT, TOK], F32R), sb("g_lo", [P, CT, TOK], F32R)
        raw = [sb(f"raw{s}", [P, CT, CW]) for s in range(2)]
        w_hi = [sb(f"w_hi{s}", [P, CT, CW], F32R) for s in range(2)]
        w_lo = [sb(f"w_lo{s}", [P, CT, CW], F32R) for s in range(2)]
        par = sb("par", [P, NPARAM])
        com = sb("com", [P, COMMON_MASKS, P])
        eps_col, eps2_col = sb("eps_col", [P, 1]), sb("eps2_col", [P, 1])
        ident, ones, halves, causal = (com[:, k, :] for k in range(COMMON_MASKS))
        sq = [sb(f"sq{k}", [P, TOK])[:] for k in range(2)]
        ss, rs, em = (sb(name, [P, TOK])[:] for name in ("ss", "rs", "em"))
        rs_col = sb("rs_col", [P, NB])
        ARENA = 20840
        arena = sb("arena", [P, ARENA])
        taken = [0]

        def part(n):
            a = arena[:, taken[0]:taken[0] + n]
            taken[0] += n
            assert taken[0] <= ARENA, taken[0]
            return a

        def fresh():
            taken[0] = 0

        fresh()
        relu_t = [part(TOK) for _ in range(2)]
        gsq = [part(TOK) for _ in range(2)]
        x_tok = part(NB * DM).rearrange("p (b n) -> p b n", b=NB)
        bias_rows = part(RW)
        rb_in = part(BIAS_COLS)
        bucket_sb = part(RW)
        bmask_sb = part(RW)

        bank = [ctx.enter_context(nc.psum_tensor(f"bank{k}", [P, TOK], F32)) for k in range(8)]
        lin_bank = bank[0:2]
        stat_bank = bank[7]

        bias_dram = nc.dram_tensor("bias_scratch", [BIAS_COLS, RW], F32, kind="Internal").ap()

        raw_loaded = [sem(f"raw_loaded{s}") for s in range(2)]
        w_hi_done, w_lo_done, lin_done = sem("w_hi_done"), sem("w_lo_done"), sem("lin_done")
        const_loaded, x_loaded = sem("const_loaded"), sem("x_loaded")
        x_turned, x_added = sem("x_turned"), sem("x_added")
        sq_done, ss_added, norm_sum = sem("sq_done"), sem("ss_added"), sem("norm_sum")
        ln_done, rs_done = sem("ln_done"), sem("rs_done")
        hh_done, hl_done = sem("hh_done"), sem("hl_done")
        relu_done, gsq_done = sem("relu_done"), sem("gsq_done")
        gh_done, gl_done = sem("gh_done"), sem("gl_done")
        copied = sem("copied")
        qsq_raw, ki_ready, gate_z = sem("qsq_raw"), sem("ki_ready"), sem("gate_z")
        qsq_done, q_evac, ssq_done = sem("qsq_done"), sem("q_evac"), sem("ssq_done")
        qln_done, qrs_done, qk_ready = sem("qln_done"), sem("qrs_done"), sem("qk_ready")
        bias_mm, bias_added, bias_saved = sem("bias_mm"), sem("bias_added"), sem("bias_saved")
        bias_loaded = [sem(f"bias_loaded{s}") for s in range(2)]
        s_done, l_done, negmax_done, p_done = sem("s_done"), sem("l_done"), sem("negmax_done"), sem("p_done")
        pt_done, pt_copied, pv_done = sem("pt_done"), sem("pt_copied"), sem("pv_done")
        rinv_done, y_done = sem("rinv_done"), sem("y_done")
        yh_done, yl_done = sem("yh_done"), sem("yl_done")
        iw_turned, iw_ready = sem("iw_turned"), sem("iw_ready")
        idx_done, idx_relu, idx_acc = sem("idx_done"), sem("idx_relu"), sem("idx_acc")
        topk_step, mask_ready, tm_done = sem("topk_step"), sem("mask_ready"), sem("tm_done")
        scaled = sem("scaled")
        out_turned, out_copied, out_saved = sem("out_turned"), sem("out_copied"), sem("out_saved")

        gate_step, gate_ln, gates_ready = sem("gate_step"), sem("gate_ln"), sem("gates_ready")
        gate_exp, cols_turned, cols_copied = sem("gate_exp"), sem("cols_turned"), sem("cols_copied")
        last_spread, cmask_loaded, col_exp = sem("last_spread"), sem("cmask_loaded"), sem("col_exp")
        conv_step, conv_done, tanh_done, silu_done = sem("conv_step"), sem("conv_done"), sem("tanh_done"), sem("silu_done")
        csq_done, csum_done, cln_done, crs_done = sem("csq_done"), sem("csum_done"), sem("cln_done"), sem("crs_done")
        qkn_done, rows_spread, age_done = sem("qkn_done"), sem("rows_spread"), sem("age_done")
        decay_done, grow_done, qe_done = sem("decay_done"), sem("grow_done"), sem("qe_done")
        kk_done, kv_turned, kv_scaled = sem("kk_done"), sem("kv_turned"), sem("kv_scaled")
        at_raw, at_done, atl_done = sem("at_raw"), sem("at_done"), sem("atl_done")
        u_done, t_turned, t_init, t_done = sem("u_done"), sem("t_turned"), sem("t_init"), sem("t_done")
        w_done, w_copied, tw_done = sem("w_done"), sem("w_copied"), sem("tw_done")
        wt_done, wt_copied = sem("wt_done"), sem("wt_copied")
        vn_done, vn_copied, ds_done, state_done = sem("vn_done"), sem("vn_copied"), sem("ds_done"), sem("state_done")
        o_done, osq_done, osum_done, oln_done, ors_done = (sem("o_done"), sem("osq_done"), sem("osum_done"),
                                                           sem("oln_done"), sem("ors_done"))
        on_done, y32_done = sem("on_done"), sem("y32_done")

        units, heads, y_first = [], [], {}
        counts = dict(s=0, t=0, v=0, y=0, tm=0)
        value = [0, 0]
        for li, i in enumerate(layers):
            y_first[i] = counts["y"]
            if KINDS[i] == 2:
                counts["y"] += C_HEADS
                continue
            kind = KINDS[i]
            for f in range(A_PAIRS if kind == 0 else B_HEADS // 2):
                for half in range(2):
                    head = 2 * f + half if kind == 0 else 8 * (f // 4) + f % 4 + 4 * half
                    H = len(heads)
                    value[H % 2] += 16 * (3 if kind == 0 else 1)
                    heads.append(dict(i=i, kind=kind, head=head, loaded=value[H % 2], f=f))
                    for b in (3, 0, 2, 1):
                        u = dict(i=i, kind=kind, f=f, half=half, head=head, b=b, H=H, u=len(units), s0=counts["s"],
                                 t0=counts["t"], v0=counts["v"])
                        if kind == 0:
                            k0 = max(0, b - 1)
                            u["pieces"] = [(0, k0, b + 1)] + [(g, 0, b + 1) for g in (1, 2)]
                        else:
                            u["pieces"] = [(0, 0, b + 1)]
                            u["tm"] = counts["tm"] if b else None
                            counts["tm"] += b > 0
                        u["blocks"] = [(g, kb) for g, ka, kz in u["pieces"] for kb in range(ka, kz)]
                        u["tp"] = -(-len(u["blocks"]) // 4)
                        counts["s"] += len(u["pieces"])
                        counts["t"] += u["tp"]
                        counts["v"] += u["tp"]
                        units.append(u)
                    heads[H]["s_end"] = counts["s"]
                heads[-1]["yt"] = counts["t"]
                heads[-1]["ylast"] = len(units)
                heads[-1]["y"] = counts["y"]
                counts["t"] += 1
                counts["y"] += 1
        last_piece_user = {u["tm"]: u["s0"] + 1 for u in units if u.get("tm") is not None}
        SKEW = {0: 1, 1: 2}

        def attention_steps(i):
            U, skew, pending = units_of(i), SKEW[KINDS[i]], None
            low = None
            for s in range(len(U) + skew):
                if s < len(U):
                    yield "scores", U[s], s
                if s < skew:
                    continue
                k = s - skew
                if k and k % 8 == 0:
                    low = pair_of(i, k // 8 - 1)
                    yield "outputs", low, s
                for p in range(U[k]["tp"]):
                    yield "turn", U[k], p
                    if low is not None:
                        yield "low", low, s
                        low = None
                    if pending is not None:
                        yield ("weigh", *pending)
                    pending = U[k], p
                if k % 8 == 7:
                    yield ("weigh", *pending)
                    pending = None
            yield "outputs", pair_of(i, U[-1]["f"]), s
            yield "low", pair_of(i, U[-1]["f"]), s

        def units_of(i):
            return [u for u in units if u["i"] == i]

        def pair_of(i, f):
            return next(h for h in heads if h["i"] == i and h["f"] == f and "yt" in h)

        q_first, copy_first, at_q, at_c = {}, {}, 0, 0
        for i in layers:
            q_first[i], copy_first[i] = at_q, at_c
            at_q += {0: 6 * A_PAIRS, 1: 10, 2: 0}[KINDS[i]]
            at_c += {0: 12, 1: 8, 2: 2 + 4 * C_HEADS}[KINDS[i]]

        evac = []
        for n, c in enumerate(CHUNKS):
            stage, i = c[:2]
            li = list(layers).index(i)
            for j in range(2):
                k = 2 * (n - first_chunk[stage, i]) + j
                if stage == "out":
                    evac.append((x_added, added(li, False) + k + 1))
                elif stage == "mlp":
                    q, k = divmod(k, 16)
                    evac.append((None, None) if k < 8 else (x_added, added(li, True) + 8 * q + k - 8 + 1))
                elif stage == "av":
                    evac.append((copied, copy_first[i] + k + 1))
                elif stage in ("aqk", "bq"):
                    evac.append((q_evac, q_first[i] + k + 1))
                elif stage == "bk":
                    evac.append((q_evac, q_first[i] + 8 + k + 1))
                elif stage in ("bkw", "bqi", "bv"):
                    evac.append((copied, copy_first[i] + k + {"bkw": 0, "bqi": 2, "bv": 6}[stage] + 1))
                elif stage == "cab":
                    evac.append((copied, copy_first[i] + k + 1))
                else:
                    evac.append((copied, copy_first[i] + 2 + k + 1))

        fresh()
        aq = [[part(TOK) for _ in range(6)] for _ in range(2)]
        av = part(NB * 3 * 512).rearrange("p (b n) -> p b n", b=NB)
        ay = part(NB * P).rearrange("p (b n) -> p b n", b=NB)
        abias = [part(sum(A_BIAS)) for _ in range(2)]
        al = [part(1280), part(768)]
        apt = [part(512) for _ in range(2)]
        asq, ars = part(TOK), part(TOK)
        ayf = part(TOK)
        small = sb("small", [P, 40])
        fresh()
        bq = [part(TOK) for _ in range(8)]
        bk = [part(TOK) for _ in range(2)]
        bv = part(NB * CW).rearrange("p (b n) -> p b n", b=NB)
        by = part(NB * P).rearrange("p (b n) -> p b n", b=NB)
        bbias = [part(TOK) for _ in range(2)]
        bl = [part(TOK) for _ in range(3)]
        bpt = [part(512) for _ in range(2)]
        bsq, brs = part(TOK), part(TOK)
        byf = part(TOK)
        bqi = [part(TOK) for _ in range(4)]
        bki = part(TOK)
        bw_row = part(TOK)
        bw = part(NB * B_IDX).rearrange("p (b n) -> p b n", b=NB)
        score = {b: part(P * (b + 1)) for b in (1, 2, 3)}
        brelu = [part(TOK) for _ in range(2)]
        btm = [part(TOK) for _ in range(2)]
        best = part(8)

        fresh()
        gc_row, beta_row = part(TOK), part(TOK)
        head_sel = part(C_HEADS * P).rearrange("p (h n) -> p h n", h=C_HEADS)
        cmask = part((NMASK - M_DECAY) * P).rearrange("p (k n) -> p k n", n=P)
        gate_in = part(2)
        neg_a = part(1)

        def cols():
            return part(NB * C_HEADS).rearrange("p (c h) -> p c h", c=NB)

        gc_col, beta_col, g_last, e_last, k_decay, beta_g = (cols() for _ in range(6))
        cx = [part(TOK) for _ in range(2)]
        cy = [[part(TOK) for _ in range(3)] for _ in range(2)]
        cg = [part(TOK) for _ in range(2)]
        cth = [part(TOK) for _ in range(2)]
        csq, ors, on = sq, em, ss
        crs = [part(TOK) for _ in range(2)]

        def four():
            return part(TOK).rearrange("p (c n) -> p c n", c=NB)

        qn, kn, qe, grow, decay, qkd, at = (four() for _ in range(7))
        atl = [four() for _ in range(3)]
        Tm, Um, Wm = four(), four(), four()
        v_beta, k_beta, k_dec, wt = four(), four(), four(), four()
        vn = [part(P) for _ in range(2)]
        state = part(P)
        m_decay, m_last = cmask[:, 0, :], cmask[:, 1, :]
        m_level = [cmask[:, 2 + k, :] for k in range(LEVELS)]
        gz, ge, gu, gl_, gd, gr = (m.rearrange("p c n -> p (c n)")[0:C_HEADS, :] for m in (*atl, Tm, Um, Wm))

        def by_block(m):
            return m.rearrange("p (b n) -> p b n", b=NB)

        def reversed_blocks(m):
            return by_block(m)[:, :, ::-1]

        INDEX_PIECES = {k: range(4 * z, 4 * z + 4) for z, k in enumerate((0, 1, 6, 7, 10, 11))}
        ROUNDS = TOPK // 8

        def norm_gain(m):
            return (G_MIX if m % 2 == 0 else G_MLP) + CT * layers[m // 2]

        def flat(m):
            return m.rearrange("p c n -> p (c n)")

        def bk4(k):
            return bank[k][:].rearrange("p (c n) -> p c n", c=NB)

        def halves_of(m, k, second):
            v = m.rearrange("p c (b z s) -> p c b z s", z=2, s=1 << k)
            return v[:, :, :, 1 if second else 0, :]

        def packed(bank_k, k):
            return bank[bank_k][:, 0:NB * 64].rearrange("p (c b s) -> p c b s", c=NB, s=1 << k)

        FILL = dict(rows=40, t=44, wt=83, vn=(85, 87, 89, 91), ds=(86, 88, 90, 92), osum=96)
        FILL_W = {k: 44 + 6 * k - 3 for k in range(1, LEVELS)}
        FILL_TW = {k: 44 + 6 * k for k in range(1, LEVELS)}

        mem = {0: dict(y=ay, l=al, pt=apt, sq=asq, rs=ars, yf=ayf, bias=abias),
               1: dict(y=by, l=bl, pt=bpt, sq=bsq, rs=brs, yf=byf, bias=bbias)}
        mx = [small[:, 4 * k:4 * k + 3] for k in range(4)]
        negmax = [small[:, 16 + k:17 + k] for k in range(4)]
        psum_of = [small[:, 20 + k:21 + k] for k in range(4)]
        rinv = [small[:, 24 + k:25 + k] for k in range(4)]

        def l_of(u):
            ring = mem[u["kind"]]["l"]
            return ring[u["u"] % len(ring)]

        def bias_of(u, g, ka, kz):
            if u["kind"] == 1 and u["b"]:
                return btm[u["tm"] % 2][:, 0:P * (kz - ka)]
            t = mem[u["kind"]]["bias"][u["H"] % 2]
            off = (0, 256, 768)[g] if u["kind"] == 0 else 0
            end = off + (A_BIAS[g] if u["kind"] == 0 else TOK)
            return t[:, end - P * (kz - ka):end]

        def qk_of(u, g):
            rows = slice(HD * u["half"], HD * u["half"] + HD)
            if u["kind"] == 0:
                q, k = aq[u["f"] % 2][2 * g], aq[u["f"] % 2][2 * g + 1]
            else:
                q, k = bq[u["f"]], bk[u["f"] // 4]
            return q[rows, :], k[rows, :]

        def v_of(u, g, kb):
            if u["kind"] == 0:
                c = (g * A_HEADS + u["head"]) * HD
                return av[:, kb, c:c + HD]
            c = (u["head"] // (B_HEADS // B_KV)) * HD
            return bv[:, kb, c:c + HD]

        def tanh_index(h, k):
            if k == 3:
                return 4 * h + 3 + (3 if h + 1 < C_HEADS else 0)
            return k if h == 0 else 4 * h - 1 + k

        def rank_in_ring(u):
            n = len(mem[u["kind"]]["l"])
            p = u["u"] - n
            return units[p] if p >= 0 and units[p]["i"] == u["i"] else None

        block = ctx.enter_context(nc.Block())

        @block.sync
        def _(sp):
            def load(n, k, dst, src):
                sp.dma_start(dst, src).then_inc(raw_loaded[n % 2], 16)

            def rows(w, c0, cols, kt=CT, r0=0):
                return w[r0:r0 + kt * P, c0:c0 + cols].rearrange("(k p) n -> p k n", p=P)

            def chunk(n):
                stage, i, k, kt, _ = CHUNKS[n]
                r = raw[n % 2]
                if n >= 2:
                    sp.wait_ge(w_lo_done, n - 1)
                if stage == "av":
                    load(n, 0, r[:], rows(a_w_in[i // 3], 3072 + k * CW, CW))
                elif stage == "aqk":
                    f, g = divmod(k, 3)
                    for s in range(2):
                        load(n, s, r[:, :, P * s:P * s + P], rows(a_w_in[i // 3], 1536 * s + 512 * g + P * f, P))
                elif stage == "out" and KINDS[i] == 1:
                    for z in range(2):
                        for s in range(2):
                            r0 = (8 * z + 4 * s) * HD
                            src = b_w_out[0][r0:r0 + 4 * HD, k * CW:(k + 1) * CW].rearrange("(t p) n -> p t n", p=HD)
                            load(n, 2 * z + s, r[HD * s:HD * s + HD, 4 * z:4 * z + 4, :], src)
                elif stage == "out":
                    w = {0: a_w_out, 1: b_w_out, 2: c_w_out}[KINDS[i]][i // 3]
                    load(n, 0, r[:, 0:kt, :], rows(w, k * CW, CW, kt))
                elif stage == "cab":
                    w = c_w_in[0]
                    for s in range(2):
                        load(n, 0, r[:, :, P * s:P * s + 8], rows(w, 4096 + 8 * s, 8))
                        load(n, 0, r[:, :, P * s + 8:P * s + P], rows(w, 0, P - 8))
                elif stage == "chd":
                    for s in range(2):
                        load(n, s, r[:, :, P * s:P * s + P], rows(c_w_in[0], DM * (2 * (k % 2) + s) + P * (k // 2), P))
                elif stage == "bkw":
                    w = b_w_in[0]
                    for s in range(2):
                        load(n, s, r[:, :, HD * s:HD * s + HD], rows(w, 2048, HD))
                    load(n, 2, r[:, :, P:P + 8], rows(w, 2112, 8))
                    load(n, 3, r[:, :, P + 8:CW], rows(w, 0, P - 8))
                elif stage == "bqi":
                    load(n, 0, r[:], rows(b_w_in[0], 1536 + k * CW, CW))
                elif stage == "bv":
                    load(n, 0, r[:], rows(b_w_in[0], 1280, CW))
                elif stage == "bk":
                    load(n, 0, r[:], rows(b_w_in[0], 1024, CW))
                elif stage == "bq":
                    for t in range(2):
                        a = 8 * (k // 2) + 2 * (k % 2) + t
                        for s in range(2):
                            c = P * t + HD * s
                            load(n, 2 * t + s, r[:, :, c:c + HD], rows(b_w_in[0], (a + 4 * s) * HD, HD))

            def mlp_chunks(i, n0, q):
                c_up = [sp.snap(q * DM + k * CW) if not isinstance(q, int) else q * DM + k * CW for k in range(4)]
                r_down = c_up[0]
                free = [sp.snap(q * 8 + (n0 + k - 1)) if not isinstance(q, int) else q * 8 + n0 + k - 1
                        for k in range(8)]
                for k in range(8):
                    if k < 4:
                        src = mlp_w1[i][:, bass.ds(c_up[k], CW)]
                    else:
                        src = mlp_w2[i][bass.ds(r_down, DM), (k - 4) * CW:(k - 3) * CW]
                    src = src.rearrange("(k p) n -> p k n", p=P)
                    if isinstance(q, int) and free[k] < 1:
                        pass
                    else:
                        sp.wait_ge(w_lo_done, free[k])
                    load(n0 + k, 0, raw[(n0 + k) % 2][:], src)

            sp.dma_start(com[:], masks[0:COMMON_MASKS * P, :].rearrange("(k p) n -> p k n", p=P)).then_inc(const_loaded, 16)
            for b in range(NB):
                sp.dma_start(x_tok[:, b, :], x_in[b * P:(b + 1) * P, :]).then_inc(x_loaded, 16)
            sp.dma_start(par[:], params).then_inc(const_loaded, 16)
            sp.dma_start(bucket_sb[0:BUCKETS, :], bucket_rows).then_inc(const_loaded, 16)
            sp.dma_start(rb_in[0:BUCKETS, :], rel_bias).then_inc(const_loaded, 16)
            sp.dma_start(bmask_sb[0:BIAS_COLS, :], bias_mask).then_inc(const_loaded, 16)
            for i in layers:
                n = min(first_chunk[s, j] for s, j in first_chunk if j == i)
                n_mlp = first_chunk["mlp", i]
                for k in range(n, n_mlp):
                    chunk(k)
                with sp.Fori(0, QUARTERS) as q:
                    mlp_chunks(i, n_mlp, q)
            for b in range(NB):
                sp.wait_ge(out_copied, 2 * b + 2)
                sp.dma_start(out[b * P:(b + 1) * P, :], x_tok[:, b, :]).then_inc(out_saved, 16)
            sp.wait_ge(out_saved, 16 * NB)

        @block.gpsimd
        def _(pool):
            def split(n, kt, value=None):
                value = n + 1 if value is None else value
                pool.wait_ge(w_hi_done, value)
                s = n % 2
                nc.gpsimd.tensor_tensor(w_lo[s][:, 0:kt, :], raw[s][:, 0:kt, :], w_hi[s][:, 0:kt, :].bitcast(F32),
                                        ALU.subtract).then_inc(w_lo_done, 1)

            def split_ahead(m):
                if m + 2 < N:
                    split(m + 2, CHUNKS[m + 2][3])

            def qk_scale(kind, Q, dst):
                pool.wait_ge(qrs_done, Q + 1)
                nc.gpsimd.tensor_tensor(dst, dst, mem[kind]["rs"], ALU.mult).then_inc(qk_ready, 1)

            def mixer_a(i):
                n0, n1, Q = first_chunk["av", i], first_chunk["aqk", i], q_first[i]
                for v in range(6):
                    split_ahead(n0 + v)
                for k in range(6):
                    if k:
                        qk_scale(0, Q + k - 1, aq[0][k - 1])
                    if k % 2:
                        split_ahead(n1 + k // 2)
                qk_scale(0, Q + 5, aq[0][5])
                for f in range(A_PAIRS - 1):
                    Q1, n2 = Q + 6 * (f + 1), n1 + 3 * (f + 1)
                    for k in range(7):
                        if k:
                            qk_scale(0, Q1 + k - 1, aq[(f + 1) % 2][k - 1])
                        if k % 2 and k < 6:
                            split_ahead(n2 + k // 2)

            def mixer_b(i):
                n0, Q = first_chunk["bkw", i], q_first[i]
                pool.wait_ge(copied, copy_first[i] + 1)
                pool.wait_ge(rs_done, 2 * list(layers).index(i) + 1)
                nc.gpsimd.tensor_tensor(bki, bki, rs, ALU.mult).then_inc(ki_ready, 1)
                for k in range(4):
                    split_ahead(n0 + k)
                dst = bq + bk
                for k in range(10):
                    if k:
                        qk_scale(1, Q + k - 1, dst[k - 1])
                    if k % 2:
                        split_ahead(n0 + 4 + k // 2)
                qk_scale(1, Q + 9, dst[9])
                for u in units_of(i):
                    if u["b"] == 0:
                        continue
                    t = u["tm"]
                    h = heads[u["H"]]
                    pool.wait_ge(bias_loaded[u["H"] % 2], h["loaded"])
                    pool.wait_ge(mask_ready, 4 - u["b"])
                    if t >= 2:
                        pool.wait_ge(l_done, last_piece_user[t - 2])
                    n = P * (u["b"] + 1)
                    nc.gpsimd.tensor_tensor(btm[t % 2][:, 0:n], bbias[u["H"] % 2][:, TOK - n:TOK],
                                            score[u["b"]], ALU.add).then_inc(tm_done, 1)

            def mixer_c(i):
                n0 = first_chunk["cab", i]
                for k in range(3):
                    split_ahead(n0 + k)
                for h in range(C_HEADS):
                    pool.wait_ge(at_done, h + 1)
                    for k in range(LEVELS):
                        if k >= 3:
                            pool.wait_ge(w_done, 6 * h + k - 3)
                        if k == 3:
                            pool.wait_ge(u_done, 7 * h + 1)
                        nc.gpsimd.tensor_tensor(atl[k % 3], at, m_level[k].unsqueeze(1).to_broadcast([P, NB, P]),
                                                ALU.mult).then_inc(atl_done, 1)
                    if h + 1 < C_HEADS:
                        split_ahead(n0 + 3 + 2 * h)
                        split_ahead(n0 + 4 + 2 * h)

            nc.gpsimd.memset(eps_col[:], EPS).then_inc(scaled, 1)
            nc.gpsimd.memset(eps2_col[:], EPS * EPS).then_inc(scaled, 1)
            for n in range(2):
                split(n, CHUNKS[n][3])
            for i in layers:
                (mixer_a, mixer_b, mixer_c)[KINDS[i]](i)
                for k in range(4):
                    split_ahead(first_chunk["out", i] + k)
                n = first_chunk["mlp", i]
                with pool.Fori(0, QUARTERS - 1) as q:
                    for k in range(8):
                        split(n + k, CT, q * 8 + (n + k + 3))
                for k in range(8):
                    split_ahead(n + 8 * (QUARTERS - 1) + k)

        @block.scalar
        def _(act):
            def rounding(n, kt, raw_v=None, lin_v=None):
                s = n % 2
                raw_v = raw_value[n] if raw_v is None else raw_v
                lin_v = 2 * n - 2 if lin_v is None else lin_v
                act.wait_ge(raw_loaded[s], raw_v)
                if not isinstance(lin_v, int) or lin_v > 0:
                    act.wait_ge(lin_done, lin_v)
                nc.scalar.activation(w_hi[s][:, 0:kt, :], raw[s][:, 0:kt, :], ACT.Copy).then_inc(w_hi_done, 1)

            def round_ahead(m):
                if m + 2 < N:
                    rounding(m + 2, CHUNKS[m + 2][3])

            def prepare(m, c, x0):
                act.wait_ge(x_added, x0 + c + 1)
                gain = norm_gain(m) + c
                nc.scalar.activation(h_hi[:, c, :], x[:, c, :], ACT.Copy, scale=par[:, gain:gain + 1]).then_inc(hh_done, 1)
                if c >= 2:
                    act.wait_ge(ss_added, 7 * m + max(1, c - 2))
                nc.scalar.activation(sq[c % 2], x[:, c, :], ACT.Square).then_inc(sq_done, 1)

            def norm(m, kind):
                act.wait_ge(norm_sum, m + 1)
                attention = kind in (0, 1)
                if attention:
                    nc.scalar.activation(em, stat_bank[:], ACT.Identity, bias=eps2_col[:], scale=EPS / DM)
                    ins = nc.scalar.activation(rs_col[:], bank[6][:, 0:NB], ACT.Ln, bias=eps_col[:], scale=1.0 / DM)
                if kind != 0:
                    ins = nc.scalar.activation(rs, stat_bank[:], ACT.Ln, bias=eps_col[:], scale=1.0 / DM)
                ins.then_inc(ln_done, 1)
                act.wait_ge(ln_done, m + 1)
                if attention:
                    ins = nc.scalar.activation(rs_col[:], rs_col[:], ACT.Exp, scale=-0.5)
                if kind != 0:
                    ins = nc.scalar.activation(rs, rs, ACT.Exp, scale=-0.5)
                ins.then_inc(rs_done, 1)

            def residual(n0, x0, m):
                for k in range(4):
                    for c in (2 * k, 2 * k + 1):
                        if m is not None:
                            prepare(m, c, x0)
                    round_ahead(n0 + k)

            def hidden(j, g):
                act.wait_ge(relu_done, g[j + 1])
                if j >= 2:
                    act.wait_ge(gl_done, g[j - 1])
                nc.scalar.activation(gsq[j % 2], relu_t[j % 2], ACT.Square).then_inc(gsq_done, 1)
                act.wait_ge(gsq_done, g[j + 1])
                nc.scalar.activation(g_hi[:, j, :], gsq[j % 2], ACT.Copy).then_inc(gh_done, 1)

            def mlp(li, i, m):
                n = first_chunk["mlp", i]
                T, G, X = 2 * n, 8 * QUARTERS * li, added(li, True)
                with act.Fori(0, QUARTERS - 1) as q:
                    t0 = [act.snap(q * 16 + (T + k)) for k in range(0, 17)]
                    g0 = {k: act.snap(q * 8 + (G + k)) for k in range(1, 9)}

                    def ahead(k):
                        v = act.snap(q * 64 + raw_value[n + k + 2])
                        rounding(n + k + 2, CT, v, t0[2 * k + 2])

                    for k in range(4):
                        for j in (2 * k, 2 * k + 1):
                            hidden(j, g0)
                        ahead(k)
                    for k in range(4, 8):
                        ahead(k)
                q = QUARTERS - 1
                G, X, n = G + 8 * q, X + 8 * q, n + 8 * q
                for k in range(4):
                    for j in (2 * k, 2 * k + 1):
                        hidden(j, {v: G + v for v in range(9)})
                    round_ahead(n + k)
                residual(n + 4, X, m)

            def copy_tile(t, dst, src, **kw):
                act.wait_ge(lin_done, t + 1)
                nc.scalar.activation(dst, src, ACT.Copy, **kw).then_inc(copied, 1)

            def qk_tile(kind, t, Q, dst, gain, query):
                src, blocks = lin_bank[t % 2][:], lambda m: m
                if query:
                    src, blocks = reversed_blocks(src), by_block
                act.wait_ge(lin_done, t + 1)
                if Q:
                    act.wait_ge(ssq_done, Q)
                nc.scalar.activation(blocks(mem[kind]["sq"]), src, ACT.Square).then_inc(qsq_raw, 1)
                nc.scalar.activation(blocks(dst), src, ACT.Copy, scale=par[:, gain:gain + 1]).then_inc(q_evac, 1)

            def values(t, c, dst):
                act.wait_ge(lin_done, t + 1)
                for z in range(2):
                    b = 2 * (t % 2) + z
                    ins = nc.scalar.activation(dst[:, b, c:c + CW], lin_bank[t % 2][:, CW * z:CW * z + CW], ACT.Copy,
                                               scale=rs_col[:, b:b + 1])
                ins.then_inc(copied, 1)

            def qk_rms(kind, Q):
                r = mem[kind]["rs"]
                act.wait_ge(ssq_done, Q + 1)
                if Q:
                    act.wait_ge(qk_ready, Q)
                nc.scalar.activation(r, stat_bank[:], ACT.Ln, bias=eps_col[:], scale=1.0 / HD).then_inc(qln_done, 1)
                act.wait_ge(qln_done, Q + 1)
                nc.scalar.activation(r, r, ACT.Exp, scale=-0.5).then_inc(qrs_done, 1)

            def load_bias(H):
                h = heads[H]
                dst = mem[h["kind"]]["bias"][H % 2]
                if h["kind"] == 0:
                    parts = [(g * A_HEADS + h["head"], (0, 256, 768)[g], A_BIAS[g]) for g in range(3)]
                else:
                    parts = [(3 * A_HEADS + h["head"], 0, TOK)]
                for row, off, n in parts:
                    src = bass.AP(bias_dram.tensor, row * RW + TOK - n, [[1, P], [1, n]])
                    nc.scalar.dma_start(dst[:, off:off + n], src).then_inc(bias_loaded[H % 2], 16)

            def probs(u):
                act.wait_ge(negmax_done, u["u"] + 1)
                n = P * len(u["blocks"])
                L = l_of(u)[:, 0:n]
                k = u["u"] % 4
                nc.scalar.activation(L, L, ACT.Exp, bias=negmax[k], accum_out=psum_of[k]).then_inc(p_done, 1)
                H = u["H"]
                if u["b"] == 1 and H + 2 < len(heads) and heads[H + 2]["i"] == u["i"]:
                    act.wait_ge(l_done, heads[H]["s_end"])
                    load_bias(H + 2)

            def y_round(h):
                act.wait_ge(pt_copied, h["yt"] + 1)
                nc.scalar.activation(g_hi[:, h["f"], :], mem[h["kind"]]["yf"], ACT.Copy).then_inc(yh_done, 1)

            def first_heads(i):
                Hs = [H for H, h in enumerate(heads) if h["i"] == i][:2]
                for H in Hs:
                    load_bias(H)

            def mixer_a(li, i):
                n0, n1, Q, U = first_chunk["av", i], first_chunk["aqk", i], q_first[i], units_of(i)
                first_heads(i)
                act.wait_ge(rs_done, 2 * li + 1)
                for v in range(6):
                    for j in range(2):
                        values(2 * (n0 + v) + j, v * CW, av)
                    round_ahead(n0 + v)
                gains = [(G_AQ, G_AK)[k % 2] + i // 3 for k in range(6)]
                for k in range(6):
                    if k:
                        qk_rms(0, Q + k - 1)
                    qk_tile(0, 2 * n1 + k, Q + k, aq[0][k], gains[k], k % 2 == 0)
                    if k % 2:
                        round_ahead(n1 + k // 2)
                qk_rms(0, Q + 5)
                for what, u, s in attention_steps(i):
                    if what == "scores":
                        probs(u)
                        f, k = s // 8, s % 8
                        Q1, n2 = Q + 6 * (f + 1), n1 + 3 * (f + 1)
                        if f + 1 < A_PAIRS and 1 <= k <= 6:
                            qk_rms(0, Q1 + k - 1)
                        if f + 1 < A_PAIRS and k < 6:
                            qk_tile(0, 2 * n2 + k, Q1 + k, aq[(f + 1) % 2][k], gains[k], k % 2 == 0)
                            if k % 2:
                                round_ahead(n2 + k // 2)
                    elif what == "outputs":
                        y_round(u)

            def copy_piece(u, p):
                n = P * min(4, len(u["blocks"]) - 4 * p)
                t = u["t0"] + p
                act.wait_ge(pt_done, t + 1)
                v = u["v0"] + p
                if v >= 2:
                    act.wait_ge(pv_done, v - 1)
                nc.scalar.activation(mem[u["kind"]]["pt"][v % 2][:, 0:n], bank[4 + t % 2][:, 0:n],
                                     ACT.Copy).then_inc(pt_copied, 1)

            def mixer_b(li, i):
                n0, Q, U = first_chunk["bkw", i], q_first[i], units_of(i)
                t0 = 2 * n0
                first_heads(i)
                act.wait_ge(rs_done, 2 * li + 1)
                copy_tile(t0, bki, lin_bank[t0 % 2][:])
                copy_tile(t0 + 1, by_block(bw_row[0:B_IDX, :]), reversed_blocks(lin_bank[1][0:B_IDX, :]),
                          scale=float(B_IDX) ** -0.5)
                round_ahead(n0)
                for k in range(4):
                    copy_tile(t0 + 2 + k, by_block(bqi[k]), reversed_blocks(lin_bank[k % 2][:]))
                    if k % 2:
                        round_ahead(n0 + 1 + k // 2)
                    if k == 0:
                        act.wait_ge(iw_turned, 1)
                        nc.scalar.activation(bw.rearrange("p b n -> p (b n)"), bank[4][:, 0:NB * B_IDX],
                                             ACT.Copy).then_inc(iw_ready, 1)
                dst = bq + bk
                for k in range(12):
                    t = t0 + 6 + k
                    for p in INDEX_PIECES.get(k, ()):
                        act.wait_ge(idx_done, p + 1)
                        if p >= 2:
                            act.wait_ge(idx_acc, p - 1)
                        n = P * (3 - p // 8 + 1)
                        nc.scalar.activation(brelu[p % 2][:, 0:n], bank[2 + p % 2][:, 0:n], ACT.Relu,
                                             scale=HD ** -0.5).then_inc(idx_relu, 1)
                        if p % 4 == 1 and k >= 3:
                            qk_rms(1, Q + k - 3)
                    if k >= 3 and k not in INDEX_PIECES:
                        qk_rms(1, Q + k - 3)
                    if k < 2:
                        values(t, 0, bv)
                    else:
                        qk_tile(1, t, Q + k - 2, dst[k - 2], G_BQ if k < 10 else G_BK, k < 10)
                    if k % 2:
                        round_ahead(n0 + 3 + k // 2)
                qk_rms(1, Q + 9)
                for what, u, p in attention_steps(i):
                    if what == "scores":
                        probs(u)
                    elif what == "turn":
                        copy_piece(u, p)
                    elif what == "outputs":
                        y_copy_round(u)

            def y_copy_round(h):
                act.wait_ge(pt_done, h["yt"] + 1)
                if h["y"]:
                    act.wait_ge(yl_done, h["y"])
                nc.scalar.activation(by_block(byf), reversed_blocks(bank[4 + h["yt"] % 2][:]), ACT.Copy).then_inc(pt_copied, 1)
                y_round(h)

            def c_tanh(i, items):
                for h, k in items:
                    n = tanh_index(h, k)
                    if n >= 2:
                        act.wait_ge(silu_done, n - 1)
                    if k < 3:
                        act.wait_ge(conv_done, 3 * h + k + 1)
                        src = cy[h % 2][k]
                    else:
                        act.wait_ge(copied, copy_first[i] + 2 + 4 * h + 4)
                        src = cg[h % 2]
                    nc.scalar.activation(cth[n % 2], src, ACT.Tanh).then_inc(tanh_done, 1)

            def mixer_c(li, i):
                n0, n1 = first_chunk["cab", i], first_chunk["chd", i]
                t0 = 2 * n0
                C8 = slice(0, C_HEADS)
                act.dma_start(cmask, masks[M_DECAY * P:, :].rearrange("(k p) n -> p k n", p=P)).then_inc(cmask_loaded, 16)
                act.dma_start(gate_in[C8, :], c_gates).then_inc(cmask_loaded, 16)
                round_ahead(n0)
                act.wait_ge(copied, copy_first[i] + 1)
                nc.scalar.activation(beta_row[C8, :], beta_row[C8, :], ACT.Tanh, scale=0.5).then_inc(gate_exp, 1)
                act.wait_ge(cmask_loaded, 32)
                act.wait_ge(gate_z, 1)
                nc.scalar.activation(ge, gz, ACT.Abs).then_inc(gate_exp, 1)
                act.wait_ge(gate_exp, 2)
                nc.scalar.activation(ge, ge, ACT.Exp, scale=-1.0).then_inc(gate_exp, 1)
                nc.scalar.activation(neg_a[C8, :], gate_in[C8, 0:1], ACT.Exp).then_inc(gate_exp, 1)
                act.wait_ge(gate_ln, 1)
                nc.scalar.activation(gl_, gu, ACT.Ln).then_inc(gate_exp, 1)
                round_ahead(n1)
                round_ahead(n1 + 1)
                c_tanh(i, [(0, 0), (0, 1), (0, 2)])
                act.wait_ge(cols_turned, 1)
                nc.scalar.activation(gc_col.rearrange("p c h -> p (c h)"), bank[2][:, 0:32], ACT.Copy).then_inc(cols_copied, 1)
                nc.scalar.activation(beta_col.rearrange("p c h -> p (c h)"), bank[3][:, 0:32], ACT.Copy).then_inc(cols_copied, 1)
                act.preload_act_table_set("natural_log_exp_and_others")
                act.wait_ge(cols_copied, 2)
                nc.scalar.activation(beta_g, gc_col, ACT.Exp).then_inc(col_exp, 1)
                act.wait_ge(last_spread, 1)
                nc.scalar.activation(e_last.rearrange("p c h -> p (c h)"), bank[4][:, 0:32], ACT.Exp).then_inc(col_exp, 1)
                act.wait_ge(col_exp, 3)
                nc.scalar.activation(k_decay, k_decay, ACT.Exp).then_inc(col_exp, 1)

                def squares(h):
                    if h >= 2:
                        act.wait_ge(osum_done, h - 1)
                    for k in range(2):
                        act.wait_ge(silu_done, tanh_index(h, k) + 1)
                        nc.scalar.activation(csq[k], cy[h % 2][k], ACT.Square).then_inc(csq_done, 1)

                def logs(h):
                    for k in range(2):
                        act.wait_ge(csum_done, 2 * h + k + 1)
                        nc.scalar.activation(crs[k], bank[3 + k][:], ACT.Ln, bias=eps_col[:]).then_inc(cln_done, 1)

                def norms(h):
                    for k in range(2):
                        act.wait_ge(cln_done, 2 * h + k + 1)
                        nc.scalar.activation(crs[k], crs[k], ACT.Exp, scale=-0.5).then_inc(crs_done, 1)

                squares(0)
                logs(0)
                norms(0)
                for h in range(C_HEADS):
                    nxt = h + 1 < C_HEADS
                    act.wait_ge(rows_spread, h + 1)
                    nc.scalar.activation(grow, bk4(2), ACT.Exp).then_inc(grow_done, 1)
                    act.wait_ge(age_done, h + 1)
                    nc.scalar.activation(decay, decay, ACT.Exp).then_inc(decay_done, 1)
                    act.wait_ge(t_turned, h + 1)
                    nc.scalar.activation(Tm, bk4(2), ACT.Copy).then_inc(t_init, 1)
                    for k in range(1, LEVELS):
                        act.wait_ge(w_done, 6 * h + k)
                        nc.scalar.activation(Wm, bk4(3), ACT.Copy).then_inc(w_copied, 1)
                        if k == 2 and nxt:
                            round_ahead(n1 + 2 * h + 2)
                    if nxt:
                        c_tanh(i, [(h + 1, 0), (h + 1, 1)])
                    act.wait_ge(wt_done, h + 1)
                    nc.scalar.activation(wt, bk4(4), ACT.Copy, scale=-1.0).then_inc(wt_copied, 1)
                    c_tanh(i, ([(h + 1, 2)] if nxt else []) + [(h, 3)])
                    for c in range(NB):
                        act.wait_ge(vn_done, 4 * h + c + 1)
                        nc.scalar.activation(vn[c % 2], bk4(5)[:, c, :], ACT.Copy).then_inc(vn_copied, 1)
                        if c == 0:
                            if nxt:
                                squares(h + 1)
                            act.preload_act_table_set("natural_log_exp_and_others")
                        if c == 1 and nxt:
                            logs(h + 1)
                        if c == 2 and nxt:
                            norms(h + 1)
                    act.wait_ge(o_done, h + 1)
                    nc.scalar.activation(csq[0], bank[2][:], ACT.Square).then_inc(osq_done, 1)
                    act.wait_ge(osum_done, h + 1)
                    nc.scalar.activation(ors, bank[3][:], ACT.Ln, bias=eps_col[:], scale=1.0 / P).then_inc(oln_done, 1)
                    act.wait_ge(oln_done, h + 1)
                    nc.scalar.activation(ors, ors, ACT.Exp, scale=-0.5).then_inc(ors_done, 1)
                    act.wait_ge(y32_done, h + 1)
                    nc.scalar.activation(g_hi[:, h, :], on, ACT.Copy).then_inc(yh_done, 1)
                    if nxt:
                        round_ahead(n1 + 2 * h + 3)

            act.preload_act_table_set("natural_log_exp_and_others")
            act.wait_ge(const_loaded, 80)
            nc.scalar.activation(par[:, G_AQ:G_AQ + 2], par[:, G_AQ:G_AQ + 2], ACT.Copy, scale=HD ** -0.5).then_inc(scaled, 1)
            nc.scalar.activation(par[:, G_BQ:G_BQ + 1], par[:, G_BQ:G_BQ + 1], ACT.Copy, scale=HD ** -0.5).then_inc(scaled, 1)
            nc.scalar.activation(par[:, G_CONV:NPARAM], par[:, G_CONV:NPARAM], ACT.Copy, scale=0.5).then_inc(scaled, 1)
            act.wait_ge(scaled, 5)
            act.wait_ge(bias_added, 1)
            nc.scalar.dma_start(bias_dram, bias_rows[0:BIAS_COLS, :]).then_inc(bias_saved, 16)
            for n in range(2):
                rounding(n, CHUNKS[n][3])
            for c in range(CT):
                prepare(0, c, 0)
            act.wait_ge(bias_saved, 16)
            for li, i in enumerate(layers):
                norm(2 * li, KINDS[i])
                (mixer_a, mixer_b, mixer_c)[KINDS[i]](li, i)
                residual(first_chunk["out", i], added(li, False), 2 * li + 1)
                norm(2 * li + 1, None)
                mlp(li, i, 2 * li + 2 if li + 1 < len(layers) else None)

        @block.vector
        def _(dve):
            def sum_square(m, c):
                if c == 0:
                    return
                dve.wait_ge(sq_done, 8 * m + c + 1)
                if c >= 2:
                    dve.wait_ge(ss_added, 7 * m + c - 1)
                nc.vector.tensor_tensor(ss, sq[0] if c == 1 else ss, sq[c % 2], ALU.add).then_inc(ss_added, 1)

            def low_x(m, c):
                gain = norm_gain(m) + c
                dve.wait_ge(hh_done, 8 * m + c + 1)
                nc.vector.scalar_tensor_tensor(h_lo[:, c, :], x[:, c, :], par[:, gain:gain + 1],
                                               h_hi[:, c, :].bitcast(F32), ALU.mult, ALU.subtract).then_inc(hl_done, 1)

            def residual(t0, x0, m):
                for c in range(CT):
                    dve.wait_ge(lin_done, t0 + c + 1)
                    nc.vector.tensor_tensor(x[:, c, :], x[:, c, :], lin_bank[(t0 + c) % 2][:], ALU.add).then_inc(x_added, 1)
                    if m is not None:
                        dve.wait_ge(x_added, x0 + c + 1)
                        low_x(m, c)
                        sum_square(m, c)

            def hidden(t, g):
                for j in range(8):
                    dve.wait_ge(lin_done, t[j + 1])
                    if j >= 2:
                        dve.wait_ge(gsq_done, g[j - 1])
                    nc.vector.scalar_tensor_tensor(relu_t[j % 2], lin_bank[j % 2][:], 0.0, rs, ALU.max,
                                                   ALU.mult).then_inc(relu_done, 1)
                    dve.wait_ge(gh_done, g[j + 1])
                    nc.vector.tensor_tensor(g_lo[:, j, :], gsq[j % 2], g_hi[:, j, :].bitcast(F32),
                                            ALU.subtract).then_inc(gl_done, 1)

            def mlp(li, i, m):
                T, G, X = 2 * first_chunk["mlp", i], 8 * QUARTERS * li, added(li, True)
                dve.wait_ge(rs_done, 2 * li + 2)
                with dve.Fori(0, QUARTERS - 1) as q:
                    g = {k: dve.snap(q * 8 + (G + k)) for k in range(1, 9)}
                    t = {k: dve.snap(q * 16 + (T + k)) for k in range(1, 17)}
                    hidden(t, g)
                    for c in range(CT):
                        dve.wait_ge(lin_done, t[8 + c + 1])
                        nc.vector.tensor_tensor(x[:, c, :], x[:, c, :], lin_bank[c % 2][:], ALU.add).then_inc(x_added, 1)
                q = QUARTERS - 1
                g = {k: G + 8 * q + k for k in range(9)}
                hidden({k: T + 16 * q + k for k in range(9)}, g)
                residual(T + 16 * q + 8, X + 8 * q, m)

            def logits(u):
                k = u["u"] % 4
                prev = rank_in_ring(u)
                if prev is not None:
                    dve.wait_ge(pt_done, prev["t0"] + prev["tp"])
                off = 0
                for p, (g, ka, kz) in enumerate(u["pieces"]):
                    n = P * (kz - ka)
                    s = u["s0"] + p
                    if p == 0:
                        if u["kind"] == 1 and u["b"]:
                            dve.wait_ge(tm_done, u["tm"] + 1)
                        else:
                            dve.wait_ge(bias_loaded[u["H"] % 2], heads[u["H"]]["loaded"])
                    dve.wait_ge(s_done, s + 1)
                    nc.vector.tensor_tensor_reduce(out=l_of(u)[:, off:off + n], in0=bank[2 + s % 2][:, 0:n],
                                                   in1=bias_of(u, g, ka, kz), scale=1.0, scalar=TAKEN, op0=ALU.add,
                                                   op1=ALU.max, accum_out=mx[k][:, p:p + 1]).then_inc(l_done, 1)
                    off += n
                dve.wait_ge(l_done, u["s0"] + len(u["pieces"]))
                nc.vector.tensor_reduce(out=negmax[k], in_=mx[k][:, 0:len(u["pieces"])], op=ALU.max, axis=AX.X,
                                        negate=True).then_inc(negmax_done, 1)

            def copy_piece(u, p):
                n = P * min(4, len(u["blocks"]) - 4 * p)
                t = u["t0"] + p
                dve.wait_ge(pt_done, t + 1)
                v = u["v0"] + p
                if v >= 2:
                    dve.wait_ge(pv_done, v - 1)
                nc.vector.tensor_copy(mem[u["kind"]]["pt"][v % 2][:, 0:n], bank[4 + t % 2][:, 0:n]).then_inc(pt_copied, 1)

            def add_eps(kind, Q, query):
                sq_, blocks, e = mem[kind]["sq"], lambda m: m, em
                if query:
                    blocks, e = by_block, reversed_blocks(em)
                dve.wait_ge(qsq_raw, Q + 1)
                nc.vector.tensor_tensor(blocks(sq_), blocks(sq_), e, ALU.add).then_inc(qsq_done, 1)

            def outputs(u):
                k = u["u"] % 4
                dve.wait_ge(p_done, u["u"] + 1)
                nc.vector.reciprocal(rinv[k], psum_of[k]).then_inc(rinv_done, 1)
                dve.wait_ge(rinv_done, u["u"] + 1)
                dve.wait_ge(pv_done, u["v0"] + u["tp"])
                nc.vector.tensor_scalar(mem[u["kind"]]["y"][:, u["b"], HD * u["half"]:HD * u["half"] + HD],
                                        bank[6][:, 0:HD], rinv[k], None, ALU.mult).then_inc(y_done, 1)

            def y_low(h):
                dve.wait_ge(yh_done, h["y"] + 1)
                nc.vector.tensor_tensor(g_lo[:, h["f"], :], mem[h["kind"]]["yf"], g_hi[:, h["f"], :].bitcast(F32),
                                        ALU.subtract).then_inc(yl_done, 1)

            def y_copy(h):
                dve.wait_ge(pt_done, h["yt"] + 1)
                if h["y"]:
                    dve.wait_ge(yl_done, h["y"])
                nc.vector.tensor_copy(by_block(ayf), reversed_blocks(bank[4 + h["yt"] % 2][:])).then_inc(pt_copied, 1)

            def mixer_a(li, i):
                Q = q_first[i]
                dve.wait_ge(rs_done, 2 * li + 1)
                for k in range(6):
                    add_eps(0, Q + k, k % 2 == 0)
                for what, u, s in attention_steps(i):
                    if what == "scores":
                        logits(u)
                        f, k = s // 8, s % 8
                        if f + 1 < A_PAIRS and 1 <= k <= 6:
                            add_eps(0, Q + 6 * (f + 1) + k - 1, k % 2 == 1)
                    elif what == "turn":
                        copy_piece(u, s)
                    elif what == "weigh" and s == u["tp"] - 1:
                        outputs(u)
                    elif what == "outputs":
                        y_copy(u)
                    elif what == "low":
                        y_low(u)

            def mixer_b(li, i):
                Q, step = q_first[i], [0]
                dve.wait_ge(rs_done, 2 * li + 1)
                dve.wait_ge(iw_ready, 1)

                def index_sums(pieces):
                    for p in pieces:
                        b, hd = 3 - p // 8, p % 8
                        n = P * (b + 1)
                        dve.wait_ge(idx_relu, p + 1)
                        w = bw[:, b, hd:hd + 1]
                        if hd == 0:
                            nc.vector.tensor_scalar(score[b], brelu[p % 2][:, 0:n], w, None, ALU.mult).then_inc(idx_acc, 1)
                        else:
                            dve.wait_ge(idx_acc, p)
                            nc.vector.scalar_tensor_tensor(score[b], brelu[p % 2][:, 0:n], w, score[b], ALU.mult,
                                                           ALU.add).then_inc(idx_acc, 1)

                def top(b, rounds):
                    if 0 in rounds:
                        dve.wait_ge(idx_acc, 8 * (4 - b))
                        nc.vector.tensor_tensor(score[b][:, P * b:P * b + P], score[b][:, P * b:P * b + P], causal,
                                                ALU.add).then_inc(topk_step, 1)
                        step[0] += 1
                    for _ in rounds:
                        dve.wait_ge(topk_step, step[0])
                        nc.vector.max(best, score[b]).then_inc(topk_step, 1)
                        dve.wait_ge(topk_step, step[0] + 1)
                        nc.vector.match_replace(out=score[b], in_to_replace=best, in_values=score[b],
                                                imm_value=TAKEN).then_inc(topk_step, 1)
                        step[0] += 2
                    if ROUNDS - 1 in rounds:
                        dve.wait_ge(topk_step, step[0])
                        nc.vector.tensor_scalar(score[b], score[b], TAKEN / 1.5, MASKED, ALU.is_gt,
                                                ALU.mult).then_inc(mask_ready, 1)

                rounds = {2: (3, range(0, 4)), 3: (3, range(4, 8)), 4: (3, range(8, 12)), 5: (3, range(12, 16)),
                          8: (2, range(0, 7)), 9: (2, range(7, 14)), 10: (2, range(14, 16))}
                for k in range(12):
                    if k in rounds:
                        top(*rounds[k])
                    index_sums(INDEX_PIECES.get(k, ()))
                    if k >= 2:
                        add_eps(1, Q + k - 2, k < 10)
                top(1, range(ROUNDS))
                for what, u, p in attention_steps(i):
                    if what == "scores":
                        logits(u)
                    elif what == "weigh" and p == u["tp"] - 1:
                        outputs(u)
                    elif what == "low":
                        y_low(u)

            def c_copy(i, h, k):
                dve.wait_ge(lin_done, 2 * first_chunk["chd", i] + 4 * h + k + 1)
                b = lin_bank[k % 2][:]
                if k < 3:
                    t = 3 * h + k
                    if t >= 2:
                        dve.wait_ge(conv_done, t - 1)
                    nc.vector.tensor_tensor(cx[t % 2], b, rs, ALU.mult).then_inc(copied, 1)
                else:
                    nc.vector.scalar_tensor_tensor(cg[h % 2], b, 0.5, rs, ALU.mult, ALU.mult).then_inc(copied, 1)

            def conv_steps(i, h, k, steps):
                t = 3 * h + k
                y, xt = cy[h % 2][k], cx[t % 2]
                for s in steps:
                    w = par[:, G_CONV + (3 - s) * 3 * C_HEADS + k * C_HEADS + h:][:, 0:1]
                    if s == 0:
                        dve.wait_ge(copied, copy_first[i] + 2 + 4 * h + k + 1)
                        nc.vector.tensor_scalar(y, xt, w, None, ALU.mult).then_inc(conv_step, 1)
                    else:
                        dve.wait_ge(conv_step, 3 * t + s)
                        nc.vector.scalar_tensor_tensor(y[:, s:], xt[:, :TOK - s], w, y[:, s:], ALU.mult,
                                                       ALU.add).then_inc(conv_step if s < 3 else conv_done, 1)

            def silu(h, k):
                n = tanh_index(h, k)
                dve.wait_ge(tanh_done, n + 1)
                y = cy[h % 2][k] if k < 3 else cg[h % 2]
                nc.vector.scalar_tensor_tensor(y, cth[n % 2], 1.0, y, ALU.add, ALU.mult).then_inc(silu_done, 1)

            def c_gates_steps(i):
                step = [0]
                C8 = slice(0, C_HEADS)

                def link(ins):
                    step[0] += 1
                    ins.then_inc(gate_step, 1)
                    dve.wait_ge(gate_step, step[0])

                dve.wait_ge(lin_done, 2 * first_chunk["cab", i] + 1)
                nc.vector.tensor_tensor(beta_row[C8, :], lin_bank[0][C8, :], rs[C8, :], ALU.mult).then_inc(copied, 1)
                dve.wait_ge(lin_done, 2 * first_chunk["cab", i] + 2)
                nc.vector.tensor_tensor(gz, lin_bank[1][C8, :], rs[C8, :], ALU.mult).then_inc(copied, 1)
                dve.wait_ge(copied, copy_first[i] + 2)
                dve.wait_ge(cmask_loaded, 32)
                nc.vector.tensor_scalar(gz, gz, gate_in[C8, 1:2], None, ALU.add).then_inc(gate_z, 1)
                c_copy(i, 0, 0)
                c_copy(i, 0, 1)
                dve.wait_ge(gate_exp, 1)
                link(nc.vector.tensor_scalar(beta_row[C8, :], beta_row[C8, :], 1.0, 0.5, ALU.add, ALU.mult))
                nc.vector.tensor_copy(head_sel[C8], ident[C8, 0:C_HEADS].unsqueeze(2).to_broadcast([C_HEADS, C_HEADS, P]))
                dve.wait_ge(gate_exp, 4)
                nc.vector.tensor_scalar(gu, ge, 1.0, None, ALU.add).then_inc(gate_ln, 1)
                dve.wait_ge(gate_ln, 1)
                link(nc.vector.tensor_scalar(gd, gu, 1.0, None, ALU.subtract))
                link(nc.vector.tensor_scalar(gr, gd, 1e-30, None, ALU.max))
                link(nc.vector.reciprocal(gr, gr))
                link(nc.vector.tensor_tensor(gr, gr, ge, ALU.mult))
                dve.wait_ge(gate_exp, 5)
                link(nc.vector.tensor_tensor(gr, gr, gl_, ALU.mult))
                link(nc.vector.scalar_tensor_tensor(gd, gd, 0.0, ge, ALU.is_equal, ALU.mult))
                link(nc.vector.tensor_tensor(gr, gr, gd, ALU.add))
                link(nc.vector.scalar_tensor_tensor(gr, gz, 0.0, gr, ALU.max, ALU.add))
                link(nc.vector.tensor_scalar(gr, gr, neg_a[C8, :], -1.0, ALU.mult, ALU.mult))
                for c in range(NB):
                    ins = nc.vector.tensor_tensor_scan(gc_row[C8, P * c:P * c + P], ones[C8, :], gr[:, P * c:P * c + P],
                                                       0.0, ALU.mult, ALU.add)
                ins.then_inc(gates_ready, 1)

            def mixer_c(li, i):
                dve.wait_ge(rs_done, 2 * li + 1)
                c_gates_steps(i)
                conv_steps(i, 0, 0, range(4))
                c_copy(i, 0, 2)
                c_copy(i, 0, 3)
                for k in (1, 2):
                    conv_steps(i, 0, k, range(4))
                for k in range(3):
                    silu(0, k)
                dve.wait_ge(col_exp, 1)
                nc.vector.tensor_tensor(beta_g, beta_g, beta_col, ALU.mult)
                dve.wait_ge(last_spread, 1)
                dve.wait_ge(col_exp, 2)
                nc.vector.tensor_tensor(k_decay, bank[4][:, 0:32].rearrange("p (c h) -> p c h", c=NB), gc_col,
                                        ALU.subtract).then_inc(col_exp, 1)

                def normed(h):
                    dve.wait_ge(crs_done, 2 * h + 2)
                    nc.vector.scalar_tensor_tensor(flat(qn), cy[h % 2][0], float(P) ** -0.5, crs[0], ALU.mult, ALU.mult)
                    nc.vector.tensor_tensor(flat(kn), cy[h % 2][1], crs[1], ALU.mult).then_inc(qkn_done, 1)

                def keys_scaled(h):
                    dve.wait_ge(kv_turned, h + 1)
                    nc.vector.tensor_tensor(v_beta, bk4(5), spread(beta_col, h), ALU.mult)
                    nc.vector.tensor_tensor(k_beta, bk4(4), spread(beta_g, h), ALU.mult)
                    if h == 0:
                        dve.wait_ge(col_exp, 4)
                    nc.vector.tensor_tensor(k_dec, bk4(4), spread(k_decay, h), ALU.mult).then_inc(kv_scaled, 1)

                def spread(col, h):
                    return col[:, :, h:h + 1].to_broadcast([P, NB, P])

                beside = {1: ((0, None), (0, (0, 1))), 2: ((0, (2, 3)), (1, None)), 3: ((1, (0, 1)),), 4: ((1, (2, 3)),),
                          5: ((2, None), (2, (0,))), 6: ((2, (1, 2, 3)),)}
                normed(0)
                keys_scaled(0)
                for h in range(C_HEADS):
                    nxt = h + 1 < C_HEADS
                    dve.wait_ge(grow_done, h + 1)
                    for c in range(NB):
                        ins = nc.vector.scalar_tensor_tensor(decay[:, c, :], bk4(2)[:, c, :], gc_col[:, c, h:h + 1],
                                                             m_decay, ALU.subtract, ALU.add)
                    ins.then_inc(age_done, 1)
                    dve.wait_ge(qkn_done, h + 1)
                    nc.vector.tensor_tensor(qe, qn, grow, ALU.mult).then_inc(qe_done, 1)
                    dve.wait_ge(kk_done, h + 1)
                    dve.wait_ge(decay_done, h + 1)
                    nc.vector.tensor_tensor(at, bk4(6), decay, ALU.mult).then_inc(at_raw, 1)
                    dve.wait_ge(at_raw, h + 1)
                    nc.vector.tensor_tensor(at, at, bk4(3), ALU.mult).then_inc(at_done, 1)
                    nc.vector.tensor_tensor(qkd, bk4(7), decay, ALU.mult)
                    dve.wait_ge(atl_done, 7 * h + 1)
                    nc.vector.tensor_tensor(Um, ident.unsqueeze(1).to_broadcast([P, NB, P]), atl[0],
                                            ALU.subtract).then_inc(u_done, 1)
                    for k in range(1, LEVELS):
                        dve.wait_ge(tw_done, 6 * h + k)
                        if k < LEVELS - 1:
                            a = halves_of(Tm, k, False)
                            nc.vector.tensor_tensor(a, a, packed(6, k), ALU.subtract).then_inc(t_done, 1)
                        a = halves_of(Um, k, True)
                        nc.vector.tensor_tensor(a, a, packed(7, k), ALU.subtract).then_inc(u_done, 1)
                        for tile, steps in beside[k] if nxt else ():
                            if steps is None:
                                c_copy(i, h + 1, tile)
                            else:
                                conv_steps(i, h + 1, tile, steps)
                    for k in range(3):
                        if nxt:
                            silu(h + 1, k)
                    for c in range(NB - 1):
                        dve.wait_ge(ds_done, 3 * h + c + 1)
                        src = bank[6 + c % 2][:, 0:P]
                        if c == 0:
                            nc.vector.tensor_copy(state, src).then_inc(state_done, 1)
                            silu(h, 3)
                        else:
                            nc.vector.scalar_tensor_tensor(state, state, e_last[:, c, h:h + 1], src, ALU.mult,
                                                           ALU.add).then_inc(state_done, 1)
                    if nxt:
                        normed(h + 1)
                    dve.wait_ge(ors_done, h + 1)
                    nc.vector.scalar_tensor_tensor(on, bank[2][:], par[:, G_CO:G_CO + 1], ors, ALU.mult,
                                                   ALU.mult).then_inc(on_done, 1)
                    dve.wait_ge(on_done, h + 1)
                    dve.wait_ge(silu_done, tanh_index(h, 3) + 1)
                    nc.vector.tensor_tensor(on, on, cg[h % 2], ALU.mult).then_inc(y32_done, 1)
                    if nxt:
                        keys_scaled(h + 1)
                    dve.wait_ge(yh_done, y_first[i] + h + 1)
                    nc.vector.tensor_tensor(g_lo[:, h, :], on, g_hi[:, h, :].bitcast(F32), ALU.subtract).then_inc(yl_done, 1)
                    if nxt:
                        c_copy(i, h + 1, 3)

            dve.wait_ge(bias_mm, 1)
            nc.vector.tensor_tensor(bias_rows[0:BIAS_COLS, 0:TOK], bank[2][0:BIAS_COLS, :], bmask_sb[0:BIAS_COLS, 0:TOK],
                                    ALU.add)
            nc.vector.tensor_tensor(bias_rows[0:BIAS_COLS, TOK:RW], bank[3][0:BIAS_COLS, 0:P],
                                    bmask_sb[0:BIAS_COLS, TOK:RW], ALU.add).then_inc(bias_added, 1)
            for c in range(CT):
                dve.wait_ge(x_turned, c + 1)
                nc.vector.tensor_copy(x[:, c, :], bank[4 + c % 2][:]).then_inc(x_added, 1)
                dve.wait_ge(x_added, c + 1)
                low_x(0, c)
                sum_square(0, c)
            for li, i in enumerate(layers):
                (mixer_a, mixer_b, mixer_c)[KINDS[i]](li, i)
                residual(2 * first_chunk["out", i], added(li, False), 2 * li + 1)
                mlp(li, i, 2 * li + 2 if li + 1 < len(layers) else None)
            for b in range(NB):
                for half in range(2):
                    k = 2 * b + half
                    dve.wait_ge(out_turned, k + 1)
                    nc.vector.tensor_copy(x_tok[:, b, half * 512:half * 512 + 512], bank[4 + k % 2][:]).then_inc(out_copied, 1)

        @block.tensor
        def _(pe):
            def product(n, t, acts, kt, lo, hi, act_sem, act0, tok):
                s, j = n % 2, t % 2
                b = lin_bank[t % 2]
                a_hi, a_lo = acts
                steps = []
                if not tok:
                    cols = slice(P * j, P * j + P)
                    for c in range(kt):
                        for w, a in ((w_hi, a_hi), (w_hi, a_lo), (w_lo, a_hi)):
                            steps.append((b[:], w[s][:, c, cols], a[:, c, :], c, len(steps) == 0, len(steps) == 3 * kt - 1))
                else:
                    for tb in (2 * j, 2 * j + 1):
                        for c in range(kt):
                            for z, (w, a) in enumerate(((w_hi, a_hi), (w_hi, a_lo), (w_lo, a_hi))):
                                steps.append((b[:, CW * (tb % 2):CW * (tb % 2) + CW], a[:, c, P * tb:P * tb + P],
                                              w[s][:, c, :], c, c + z == 0, c == kt - 1 and z == 2))
                lo, hi = lo * len(steps) // 24, hi * len(steps) // 24
                if lo == 0:
                    pe.wait_ge(w_lo_done, n + 1)
                    if t >= 2 and evac[t - 2][0] is not None:
                        pe.wait_ge(*evac[t - 2])
                for k in range(lo, hi):
                    o, lhsT, rhs, c, start, stop = steps[k]
                    if act_sem is not None and (k == 0 or steps[k - 1][3] < c) :
                        pe.wait_ge(act_sem, act0 + c + 1)
                    mm = nc.tensor.matmul(o, lhsT, rhs, start=start, stop=stop)
                if hi == len(steps):
                    mm.then_inc(lin_done, 1)

            H = (h_hi, h_lo)

            def norm(m, columns=False):
                pe.wait_ge(ss_added, 7 * (m + 1))
                mm = nc.tensor.matmul(stat_bank[:], ones, ss, start=True, stop=True)
                if columns:
                    for b in range(NB):
                        mm = nc.tensor.matmul(bank[6][:, b:b + 1], ss[:, P * b:P * b + P], ones[:, 0:1], start=True,
                                              stop=True)
                mm.then_inc(norm_sum, 1)

            def out_ahead(i, j, lo, hi):
                n0 = first_chunk["out", i]
                kt = CHUNKS[n0][3]
                assert hi <= 24 * (kt - 1) // kt
                product(n0, 2 * n0 + j, (g_hi, g_lo), kt, lo, hi, yl_done, y_first[i], None)

            def out_proj(li, i):
                n0 = first_chunk["out", i]
                kt = CHUNKS[n0][3]
                for k in range(4):
                    for j in range(2):
                        lo = 24 * (kt - 1) // kt if k == 0 else 0
                        product(n0 + k, 2 * (n0 + k) + j, (g_hi, g_lo), kt, lo, 24, yl_done, y_first[i], None)

            def mlp_quarter(n, v_h, v_lo, v_x, v_relu, v_g):
                for k in range(8):
                    s = (n + k) % 2
                    for j in range(2):
                        t = 2 * k + j
                        if j == 0:
                            pe.wait_ge(w_lo_done, v_lo[k])
                        if t < 2:
                            pe.wait_ge(x_added, v_x[t - 1])
                        elif t < 10:
                            pe.wait_ge(relu_done, v_relu[t - 1])
                        else:
                            pe.wait_ge(x_added, v_x[t - 9])
                        a_hi, a_lo = (h_hi, h_lo) if k < 4 else (g_hi, g_lo)
                        for c in range(CT):
                            if k == 0 and j == 0:
                                pe.wait_ge(hl_done, v_h + c + 1)
                            if k == 4 and j == 0:
                                pe.wait_ge(gl_done, v_g[c + 1])
                            for z, (w, a) in enumerate(((w_hi, a_hi), (w_hi, a_lo), (w_lo, a_hi))):
                                mm = nc.tensor.matmul(lin_bank[j][:], w[s][:, c, P * j:P * j + P], a[:, c, :],
                                                      start=c + z == 0, stop=c == CT - 1 and z == 2)
                        mm.then_inc(lin_done, 1)

            def mlp(li, i):
                n = first_chunk["mlp", i]
                G, X = 8 * QUARTERS * li, added(li, True)
                with pe.Fori(0, QUARTERS) as q:
                    v_lo = [pe.snap(q * 8 + (n + k + 1)) for k in range(8)]
                    v_x = {k: pe.snap(q * 8 + (X + k)) for k in range(-1, 7)}
                    v_g = {k: pe.snap(q * 8 + (G + k)) for k in range(1, 9)}
                    mlp_quarter(n, 8 * (2 * li + 1), v_lo, v_x, v_g, v_g)

            def scores(u):
                for p, (g, ka, kz) in enumerate(u["pieces"]):
                    s = u["s0"] + p
                    q, k = qk_of(u, g)
                    if u["kind"] == 0:
                        pe.wait_ge(qk_ready, q_first[u["i"]] + 6 * u["f"] + 2 * g + 2)
                    if s >= 2:
                        pe.wait_ge(l_done, s - 1)
                    b = u["b"]
                    nc.tensor.matmul(bank[2 + s % 2][:, 0:P * (kz - ka)], q[:, P * b:P * b + P], k[:, P * ka:P * kz],
                                     start=True, stop=True).then_inc(s_done, 1)

            def turn(u, p):
                t = u["t0"] + p
                nb = min(4, len(u["blocks"]) - 4 * p)
                if p == 0:
                    pe.wait_ge(p_done, u["u"] + 1)
                if t >= 2:
                    pe.wait_ge(pt_copied, t - 1)
                for k in range(nb):
                    c = P * (4 * p + k)
                    mm = nc.tensor.transpose(bank[4 + t % 2][:, P * k:P * k + P], l_of(u)[:, c:c + P], ident)
                mm.then_inc(pt_done, 1)

            def weigh(u, p):
                t = u["t0"] + p
                pe.wait_ge(pt_copied, t + 1)
                if p == 0 and u["u"]:
                    pe.wait_ge(y_done, u["u"])
                nb = len(u["blocks"])
                for k in range(4 * p, min(4 * p + 4, nb)):
                    g, kb = u["blocks"][k]
                    mm = nc.tensor.matmul(bank[6][:, 0:HD], mem[u["kind"]]["pt"][(u["v0"] + p) % 2][:, P * (k % 4):P * (k % 4) + P],
                                          v_of(u, g, kb), start=k == 0, stop=k == nb - 1)
                mm.then_inc(pv_done, 1)

            def turn_outputs(h):
                pe.wait_ge(y_done, h["ylast"])
                pe.wait_ge(pt_copied, h["yt"] - 1)
                y = mem[h["kind"]]["y"]
                for b in range(NB):
                    mm = nc.tensor.transpose(bank[4 + h["yt"] % 2][:, P * b:P * b + P], y[:, b, :], ident)
                mm.then_inc(pt_done, 1)

            def sum_qk(kind, Q):
                pe.wait_ge(qsq_done, Q + 1)
                if Q:
                    pe.wait_ge(qln_done, Q)
                nc.tensor.matmul(stat_bank[:], halves, mem[kind]["sq"], start=True, stop=True).then_inc(ssq_done, 1)

            def attention(i, fill):
                step, part, parts = 0, 0, 1
                for what, u, s in attention_steps(i):
                    if what == "scores":
                        step, part = s, 0
                        U = units_of(i)
                        parts = 1 + (U[s - SKEW[KINDS[i]]]["tp"] if s >= SKEW[KINDS[i]] else 0)
                        scores(u)
                        fill(step, part, parts)
                    elif what == "turn":
                        turn(u, s)
                    elif what == "weigh":
                        weigh(u, s)
                    elif what == "outputs":
                        turn_outputs(u)
                    if what == "turn":
                        part += 1
                        fill(step, part, parts)

            def mixer_a(li, i):
                n0, n1, Q = first_chunk["av", i], first_chunk["aqk", i], q_first[i]
                for v in range(6):
                    for j in range(2):
                        product(n0 + v, 2 * (n0 + v) + j, H, CT, 0, 24, hl_done if v == 0 else None, 16 * li, "pair")
                        if v + j == 0:
                            norm(2 * li, True)

                def tile(n, k, lo, hi):
                    product(n + k // 2, 2 * n + k, H, CT, lo, hi, None, 0, None)

                for k in range(6):
                    tile(n1, k, 0, 12)
                    if k:
                        sum_qk(0, Q + k - 1)
                    tile(n1, k, 12, 24)
                sum_qk(0, Q + 5)
                pe.wait_ge(copied, copy_first[i] + 12)

                def fill(s, part, parts):
                    f, k = s // 8, s % 8
                    if s >= 8 * A_PAIRS:
                        return
                    if f + 1 == A_PAIRS:
                        if part == 0 and k >= 2:
                            out_ahead(i, (k - 2) // 3, 6 * ((k - 2) % 3), 6 * ((k - 2) % 3) + 6)
                        return
                    Q1, n2 = Q + 6 * (f + 1), n1 + 3 * (f + 1)
                    if part == min(1, parts - 1) and 1 <= k <= 6:
                        sum_qk(0, Q1 + k - 1)
                    if k < 6:
                        tile(n2, k, 24 * part // parts, 24 * (part + 1) // parts)

                attention(i, fill)

            def mixer_b(li, i):
                n0, Q = first_chunk["bkw", i], q_first[i]
                t0 = 2 * n0
                product(n0, t0, H, CT, 0, 24, hl_done, 16 * li, None)
                norm(2 * li, True)
                product(n0, t0 + 1, H, CT, 0, 24, None, 0, None)
                for k in range(4):
                    product(n0 + 1 + k // 2, t0 + 2 + k, H, CT, 0, 24, None, 0, None)
                    if k == 0:
                        pe.wait_ge(copied, copy_first[i] + 2)
                        for b in range(NB):
                            mm = nc.tensor.transpose(bank[4][:, B_IDX * b:B_IDX * b + B_IDX],
                                                     bw_row[0:B_IDX, P * b:P * b + P], ident[0:B_IDX, 0:B_IDX])
                        mm.then_inc(iw_turned, 1)
                pe.wait_ge(copied, copy_first[i] + 6)
                pe.wait_ge(ki_ready, 1)
                for k in range(12):
                    t, n = t0 + 6 + k, n0 + 3 + k // 2
                    for z in range(4):
                        if k in INDEX_PIECES:
                            p = INDEX_PIECES[k][z]
                            b, hd = 3 - p // 8, p % 8
                            if p >= 2:
                                pe.wait_ge(idx_relu, p - 1)
                            r = slice(HD * (hd % 2), HD * (hd % 2) + HD)
                            nc.tensor.matmul(bank[2 + p % 2][:, 0:P * (b + 1)], bqi[hd // 2][r, P * b:P * b + P],
                                             bki[r, 0:P * (b + 1)], start=True, stop=True).then_inc(idx_done, 1)
                        if z == 2 and k >= 3:
                            sum_qk(1, Q + k - 3)
                        product(n, t, H, CT, 6 * z, 6 * z + 6, None, 0, "pair" if k < 2 else None)
                sum_qk(1, Q + 9)
                pe.wait_ge(qk_ready, Q + 10)
                pe.wait_ge(idx_relu, 24)

                def fill(s, part, parts):
                    k = s - 8 * (B_HEADS // 2 - 1)
                    if part == 0 and 0 <= k < 8:
                        out_ahead(i, k // 4, 6 * (k % 4), min(6 * (k % 4) + 6, 21))

                attention(i, fill)

            def mixer_c(li, i):
                n0, n1 = first_chunk["cab", i], first_chunk["chd", i]
                C8 = slice(0, C_HEADS)
                product(n0, 2 * n0, H, CT, 0, 24, hl_done, 16 * li, None)
                norm(2 * li)
                product(n0, 2 * n0 + 1, H, CT, 0, 24, None, 0, None)

                def fill(h, lo, hi):
                    if h == C_HEADS:
                        for j in range(2):
                            a, z = (min(max(v - 48 * j, 0), 48) * 21 // 48 for v in (lo, hi))
                            if a < z:
                                out_ahead(i, j, a, z)
                    else:
                        for k in range(4):
                            a, z = max(lo, 24 * k), min(hi, 24 * k + 24)
                            if a < z:
                                product(n1 + 2 * h + k // 2, 2 * n1 + 4 * h + k, H, CT, a - 24 * k, z - 24 * k, None, 0, None)

                fill(0, 0, 96)
                pe.wait_ge(gates_ready, 1)
                for k, rows in enumerate((gc_row, beta_row)):
                    for c in range(NB):
                        mm = nc.tensor.transpose(bank[2 + k][:, C_HEADS * c:C_HEADS * c + C_HEADS],
                                                 rows[C8, P * c:P * c + P], ident[C8, C8])
                mm.then_inc(cols_turned, 1)
                pe.wait_ge(cols_copied, 2)
                pe.wait_ge(cmask_loaded, 32)
                nc.tensor.matmul(bank[4][:, 0:32], m_last, gc_col.rearrange("p c h -> p (c h)"), start=True,
                                 stop=True).then_inc(last_spread, 1)

                def norm_sums(h):
                    for k in range(2):
                        pe.wait_ge(csq_done, 2 * h + k + 1)
                        if k == 1:
                            pe.wait_ge(wt_copied, h) if h else pe.wait_ge(col_exp, 3)
                        nc.tensor.matmul(bank[3 + k][:], ones, csq[k], start=True, stop=True).then_inc(csum_done, 1)

                def key_products(h):
                    pe.wait_ge(qkn_done, h + 1)
                    for c in range(NB):
                        nc.tensor.matmul(bk4(6)[:, c, :], kn[:, c, :], kn[:, c, :], start=True, stop=True)
                    for c in range(NB):
                        mm = nc.tensor.matmul(bk4(7)[:, c, :], kn[:, c, :], qn[:, c, :], start=True, stop=True)
                    mm.then_inc(kk_done, 1)

                def turn_keys(h):
                    for c in range(NB):
                        nc.tensor.transpose(bk4(4)[:, c, :], kn[:, c, :], ident)
                    pe.wait_ge(silu_done, tanh_index(h, 2) + 1)
                    for c in range(NB):
                        mm = nc.tensor.transpose(bk4(5)[:, c, :], cy[h % 2][2][:, P * c:P * c + P], ident)
                    mm.then_inc(kv_turned, 1)

                norm_sums(0)
                key_products(0)
                turn_keys(0)
                for h in range(C_HEADS):
                    at_ = [0]

                    def filler(to):
                        fill(h + 1, at_[0], to)
                        at_[0] = to

                    if h:
                        pe.wait_ge(on_done, h)
                    nc.tensor.matmul(bank[2][:], head_sel[C8, h, :], gc_row[C8, :], start=True, stop=True)
                    nc.tensor.matmul(bank[3][:], head_sel[C8, h, :], beta_row[C8, :], start=True,
                                     stop=True).then_inc(rows_spread, 1)
                    filler(FILL["rows"])
                    pe.wait_ge(u_done, 7 * h + 1)
                    for c in range(NB):
                        mm = nc.tensor.transpose(bk4(2)[:, c, :], Um[:, c, :], ident)
                    mm.then_inc(t_turned, 1)
                    filler(FILL["t"])
                    for k in range(1, LEVELS):
                        if k == 1:
                            pe.wait_ge(t_init, h + 1)
                        else:
                            pe.wait_ge(t_done, 5 * h + k - 1)
                        pe.wait_ge(atl_done, 7 * h + k + 1)
                        for c in range(NB):
                            mm = nc.tensor.matmul(bk4(3)[:, c, :], atl[k % 3][:, c, :], Tm[:, c, :], start=True, stop=True)
                        mm.then_inc(w_done, 1)
                        filler(FILL_W[k])
                        pe.wait_ge(w_copied, 6 * h + k)
                        pe.wait_ge(u_done, 7 * h + k)
                        for c in range(NB):
                            if k < LEVELS - 1:
                                nc.tensor.matmul(packed(6, k)[:, c], Um[:, c, :], halves_of(Wm, k, False)[:, c],
                                                 start=True, stop=True)
                        for c in range(NB):
                            mm = nc.tensor.matmul(packed(7, k)[:, c], Wm[:, c, :], halves_of(Um, k, True)[:, c],
                                                  start=True, stop=True)
                        mm.then_inc(tw_done, 1)
                        filler(FILL_TW[k])
                    pe.wait_ge(u_done, 7 * h + 7)
                    pe.wait_ge(kv_scaled, h + 1)
                    for c in range(NB):
                        mm = nc.tensor.matmul(bk4(4)[:, c, :], k_beta[:, c, :], Um[:, c, :], start=True, stop=True)
                    mm.then_inc(wt_done, 1)
                    filler(FILL["wt"])
                    for c in range(NB):
                        mm = nc.tensor.matmul(bk4(5)[:, c, :], Um[:, c, :], v_beta[:, c, :], start=True, stop=c == 0)
                        if c:
                            if c == 1:
                                pe.wait_ge(wt_copied, h + 1)
                            pe.wait_ge(state_done, 3 * h + c)
                            mm = nc.tensor.matmul(bk4(5)[:, c, :], wt[:, c, :], state, start=False, stop=True)
                        mm.then_inc(vn_done, 1)
                        if c:
                            nc.tensor.matmul(bk4(2)[:, c, :], state, qe[:, c, :], start=True, stop=False)
                        filler(FILL["vn"][c])
                        if c == 1 and h + 1 < C_HEADS:
                            norm_sums(h + 1)
                        pe.wait_ge(vn_copied, 4 * h + c + 1)
                        mm = nc.tensor.matmul(bk4(2)[:, c, :], vn[c % 2], qkd[:, c, :], start=c == 0, stop=True)
                        if c == NB - 1:
                            mm.then_inc(o_done, 1)
                        else:
                            nc.tensor.matmul(bank[6 + c % 2][:, 0:P], k_dec[:, c, :], vn[c % 2], start=True,
                                             stop=True).then_inc(ds_done, 1)
                        filler(FILL["ds"][c])
                    if h + 1 < C_HEADS:
                        key_products(h + 1)
                    pe.wait_ge(osq_done, h + 1)
                    nc.tensor.matmul(bank[3][:], ones, csq[0], start=True, stop=True).then_inc(osum_done, 1)
                    filler(FILL["osum"])
                    if h + 1 < C_HEADS:
                        turn_keys(h + 1)

            pe.wait_ge(const_loaded, 80)
            for k, (a, z) in enumerate(((0, TOK), (TOK, RW))):
                mm = nc.tensor.matmul(bank[2 + k][0:BIAS_COLS, 0:z - a], rb_in[0:BUCKETS, :], bucket_sb[0:BUCKETS, a:z],
                                      start=True, stop=True)
            mm.then_inc(bias_mm, 1)
            pe.wait_ge(x_loaded, 16 * NB)
            for c in range(CT):
                if c >= 2:
                    pe.wait_ge(x_added, c - 1)
                for b in range(NB):
                    mm = nc.tensor.transpose(bank[4 + c % 2][:, P * b:P * b + P], x_tok[:, b, P * c:P * c + P], ident)
                mm.then_inc(x_turned, 1)
            for li, i in enumerate(layers):
                (mixer_a, mixer_b, mixer_c)[KINDS[i]](li, i)
                out_proj(li, i)
                norm(2 * li + 1)
                mlp(li, i)
            pe.wait_ge(x_added, added(len(layers), False))
            for b in range(NB):
                for half in range(2):
                    k = 2 * b + half
                    if k >= 2:
                        pe.wait_ge(out_copied, k - 1)
                    for c in range(4):
                        mm = nc.tensor.transpose(bank[4 + k % 2][:, P * c:P * c + P],
                                                 x[:, 4 * half + c, P * b:P * b + P], ident)
                    mm.then_inc(out_turned, 1)


def t5_bucket(dist):
    exact = BUCKETS // 2
    d = np.maximum(dist, 1).astype(np.float32)
    part = np.log(d / np.float32(exact)) / np.float32(math.log(2048 / exact)) * np.float32(BUCKETS - exact)
    large = np.minimum(exact + part.astype(np.int32), BUCKETS - 1)
    return np.where(dist < exact, dist, large)


def constants():
    r, c = np.arange(P)[:, None], np.arange(P)[None, :]
    masks = np.zeros((NMASK, P, P), np.float32)
    masks[M_ID] = r == c
    masks[M_ONES] = 1.0
    masks[M_HALVES] = r // HD == c // HD
    masks[M_CAUSAL] = np.where(c > P - 1 - r, MASKED, 0.0)
    masks[M_DECAY] = np.where(r > c, MASKED, 0.0)
    masks[M_LAST] = (r == P - 1) * np.ones((1, P))
    for k in range(LEVELS):
        s = 1 << k
        masks[M_LEVEL + k] = (r // (2 * s) == c // (2 * s)) & (r % (2 * s) < s) & (c % (2 * s) >= s)
    dist = TOK - 1 - np.arange(RW)
    rows = np.zeros((BUCKETS, RW), np.float32)
    rows[t5_bucket(np.maximum(dist, 0)), np.arange(RW)] = dist >= 0
    mask = np.zeros((BIAS_COLS, RW), np.float32)
    for g, (window, dilation) in enumerate(A_GROUPS):
        ok = (dist >= 0) & (dist <= window) & (dist % dilation == 0)
        mask[g * A_HEADS:(g + 1) * A_HEADS] = np.where(ok, 0.0, MASKED)
    mask[len(A_GROUPS) * A_HEADS:] = np.where(dist >= 0, 0.0, MASKED)
    return masks.reshape(NMASK * P, P), rows, mask


def columns(v, times=1):
    v = np.asarray(v)
    return np.concatenate([v.reshape(-1, v.shape[-1])] * times, axis=1).reshape(-1, P).T


def layout(inputs):
    masks, bucket_rows, bias_mask = constants()
    params = np.concatenate([
        columns(inputs["norm_mix"]), columns(inputs["norm_mlp"]),
        columns(inputs["a_q_gain"], 2), columns(inputs["a_k_gain"], 2),
        columns(inputs["b_q_gain"], 2), columns(inputs["b_k_gain"], 2),
        columns(inputs["c_o_gain"]), columns(inputs["c_conv_w"]),
    ], axis=1)
    gates = np.concatenate([np.asarray(inputs["c_a_log"]).T, np.asarray(inputs["c_dt_bias"]).T], axis=1)
    arrays = {
        "x_in": np.asarray(inputs["x"])[0], "rel_bias": inputs["rel_bias"], "params": params, "c_gates": gates,
        "masks": masks, "bucket_rows": bucket_rows, "bias_mask": bias_mask,
    }
    for name in ("mlp_w1", "mlp_w2", "a_w_in", "a_w_out", "b_w_in", "b_w_out", "c_w_in", "c_w_out"):
        arrays[name] = inputs[name]
    return {k: np.ascontiguousarray(v) for k, v in arrays.items()}


def kernel(**inputs):
    import concourse.bacc as bacc
    from concourse.bass_utils import run_bass_kernel_spmd

    nc = bacc.Bacc("TRN2", target_bir_lowering=False, num_devices=1, dynamic_dma_scratch_size=1024)
    arrays = layout(inputs)
    aps = {k: nc.dram_tensor(f"in_{k}", v.shape, mybir.dt.from_np(v.dtype), kind="ExternalInput").ap()
           for k, v in arrays.items()}
    out = nc.dram_tensor("out_y", (TOK, DM), F32, kind="ExternalOutput").ap()
    trunk(nc, out=out, **aps)
    r = run_bass_kernel_spmd(nc, [{f"in_{k}": v for k, v in arrays.items()}], core_ids=[0])
    return r.results[0]["out_y"].reshape(1, TOK, DM)
```
